# Optimizing a Trainium2 kernel written in Bass

```python
import math
import jax, jax.numpy as jnp
from jax import lax
import numpy as np

D_MODEL = 1024
BATCH = 1
SEQ = 2048
DEPTH = 1
DEC_BATCH = 8
DEC_SEQ = 1
PAST_LEN = 16384
PAGE_SIZE = 128

ML_HEADS = 4
ML_DK = D_MODEL // 8
ML_DV = D_MODEL // 8
ML_WIDTH = ML_HEADS * ML_DV
ML_QK_WIDTH = ML_HEADS * ML_DK
ML_CHUNK = 128
CM_HEADS = 4
CM_HEAD_DIM = D_MODEL // 8
CM_WIDTH = CM_HEADS * CM_HEAD_DIM
CM_CHUNK = 128
MIX_WIDTH = ML_WIDTH + CM_WIDTH
IN_SIZES = (ML_QK_WIDTH, ML_QK_WIDTH, ML_WIDTH, ML_WIDTH, ML_HEADS, ML_HEADS, CM_WIDTH, CM_WIDTH)
N_IN = sum(IN_SIZES)
D_FF = -(-8 * D_MODEL // (3 * 256)) * 256
N_MOD = 6
EPS = 1e-6

kernel_name = "hybrid_mlstm_chunkmlp_decode_step"

def rmsnorm(x, g):
    x32 = x.astype(jnp.float32)
    y = x32 * lax.rsqrt(jnp.mean(x32 * x32, axis=-1, keepdims=True) + EPS)
    return (y * g.astype(jnp.float32)).astype(x.dtype)

def layernorm(x, g, b):
    x32 = x.astype(jnp.float32)
    mu = jnp.mean(x32, axis=-1, keepdims=True)
    var = jnp.mean(jnp.square(x32 - mu), axis=-1, keepdims=True)
    y = (x32 - mu) * lax.rsqrt(var + EPS)
    return (y * g.astype(jnp.float32) + b.astype(jnp.float32)).astype(x.dtype)

def split_cols(a, sizes):
    idx = np.cumsum(sizes)[:-1].tolist()
    return jnp.split(a, idx, axis=-1)

def mlstm_chunkwise(q, k, v, i_pre, f_pre, C0, n0, m0):
    B, T, H, _ = q.shape
    L = math.gcd(T, ML_CHUNK)
    nc = T // L

    def to_chunks(a):
        a = a.reshape((B, nc, L) + a.shape[2:])
        a = jnp.moveaxis(a, 3, 2)
        return jnp.moveaxis(a, 1, 0)

    qc = to_chunks(q) * (ML_DK ** -0.5)
    kc = to_chunks(k)
    vc = to_chunks(v)
    ic = to_chunks(i_pre)
    lfc = jax.nn.log_sigmoid(to_chunks(f_pre))
    causal = jnp.tril(jnp.ones((L, L), dtype=bool))

    def step(carry, xs):
        C, n, m = carry
        qb, kb, vb, ib, lfb = xs
        b = jnp.cumsum(lfb, axis=-1)
        D = jnp.where(causal, b[..., :, None] - b[..., None, :] + ib[..., None, :], -jnp.inf)
        inter = b + m[..., None]
        m_t = jnp.maximum(inter, jnp.max(D, axis=-1))
        w_intra = jnp.exp(D - m_t[..., None])
        w_inter = jnp.exp(inter - m_t)
        s = jnp.einsum('bhtd,bhsd->bhts', qb, kb) * w_intra
        num = jnp.einsum('bhts,bhse->bhte', s, vb) + w_inter[..., None] * jnp.einsum('bhed,bhtd->bhte', C, qb)
        den = jnp.sum(s, axis=-1) + w_inter * jnp.einsum('bhd,bhtd->bht', n, qb)
        h = num / jnp.maximum(jnp.abs(den), jnp.exp(-m_t))[..., None]
        g = b[..., -1:] - b + ib
        dec = b[..., -1] + m
        m_new = jnp.maximum(dec, jnp.max(g, axis=-1))
        wg = jnp.exp(g - m_new[..., None])
        wd = jnp.exp(dec - m_new)
        C_new = wd[..., None, None] * C + jnp.einsum('bhs,bhse,bhsd->bhed', wg, vb, kb)
        n_new = wd[..., None] * n + jnp.einsum('bhs,bhsd->bhd', wg, kb)
        return (C_new, n_new, m_new), h

    (C, n, m), h = lax.scan(step, (C0, n0, m0), (qc, kc, vc, ic, lfc))
    h = jnp.moveaxis(h, 0, 1)
    h = jnp.moveaxis(h, 2, 3).reshape(B, T, H, -1)
    return h, C, n, m

def chunk_spatial_gate(u, v, w_s, b_s):
    B, T = v.shape[:2]
    Tp = -(-T // CM_CHUNK) * CM_CHUNK
    vp = jnp.pad(v, ((0, 0), (0, Tp - T), (0, 0), (0, 0)))
    vp = vp.reshape(B, Tp // CM_CHUNK, CM_CHUNK, CM_HEADS, CM_HEAD_DIM)
    w = jnp.where(jnp.tril(jnp.ones((CM_CHUNK, CM_CHUNK), dtype=bool))[None], w_s, jnp.zeros_like(w_s))
    s = jnp.einsum('hts,bcshe->bcthe', w, vp) + jnp.transpose(b_s)[None, None, :, :, None]
    s = s.reshape(B, Tp, CM_HEADS, CM_HEAD_DIM)[:, :T]
    return u * s

def hybrid_layer(x, c, C0, n0, m0, w_ada, b_ada, g_norm1, w_in, b_gate, g_mlstm_head,
                 ln_v_g, ln_v_b, w_s, b_s, w_out, g_norm2, w_gate_up, w_down):
    B, T, _ = x.shape
    mod = jax.nn.silu(c) @ w_ada + b_ada
    sh1, sc1, gt1, sh2, sc2, gt2 = [m_[:, None, :] for m_ in jnp.split(mod, N_MOD, axis=-1)]

    h = rmsnorm(x, g_norm1) * (1 + sc1) + sh1
    proj = h @ w_in
    q, k, vm, o, ig, fg, u, vs = split_cols(proj, IN_SIZES)
    f32 = jnp.float32
    q = q.reshape(B, T, ML_HEADS, ML_DK).astype(f32)
    k = k.reshape(B, T, ML_HEADS, ML_DK).astype(f32)
    vm = vm.reshape(B, T, ML_HEADS, ML_DV).astype(f32)
    i_pre = ig.astype(f32) + b_gate[:ML_HEADS].astype(f32)
    f_pre = fg.astype(f32) + b_gate[ML_HEADS:].astype(f32)
    h_ml, C, n, m = mlstm_chunkwise(q, k, vm, i_pre, f_pre,
                                    C0.astype(f32), n0.astype(f32), m0.astype(f32))
    h_ml = rmsnorm(h_ml.astype(x.dtype), g_mlstm_head)
    h_ml = h_ml * jax.nn.sigmoid(o.reshape(B, T, ML_HEADS, ML_DV))

    u = jax.nn.gelu(u).reshape(B, T, CM_HEADS, CM_HEAD_DIM)
    vs = layernorm(jax.nn.gelu(vs).reshape(B, T, CM_HEADS, CM_HEAD_DIM), ln_v_g, ln_v_b)
    h_cm = chunk_spatial_gate(u, vs, w_s, b_s)

    mix = jnp.concatenate([h_ml.reshape(B, T, ML_WIDTH), h_cm.reshape(B, T, CM_WIDTH)], axis=-1)
    x = x + gt1 * (mix @ w_out)

    h2 = rmsnorm(x, g_norm2) * (1 + sc2) + sh2
    a, bb = jnp.split(h2 @ w_gate_up, 2, axis=-1)
    x = x + gt2 * ((jax.nn.silu(a) * bb) @ w_down)
    return x, C, n, m, vs

def setup_inputs(seed: int = 0) -> dict:
    key = jax.random.key(seed)
    ks = jax.random.split(key, 24)
    f = jnp.float32
    nrm = lambda k_, s: jax.random.normal(k_, s, f)
    inp = {}
    inp['x_prompt'] = nrm(ks[0], (BATCH, SEQ, D_MODEL))
    inp['x_sample'] = nrm(ks[1], (DEC_BATCH, DEC_SEQ, D_MODEL))
    inp['c_prompt'] = nrm(ks[2], (BATCH, D_MODEL))
    inp['c_sample'] = nrm(ks[3], (DEC_BATCH, D_MODEL))
    inp['state_mlstm_C'] = 0.5 * nrm(ks[4], (DEPTH, DEC_BATCH, ML_HEADS, ML_DV, ML_DK))
    inp['state_mlstm_n'] = 0.5 * nrm(ks[5], (DEPTH, DEC_BATCH, ML_HEADS, ML_DK))
    inp['state_mlstm_m'] = nrm(ks[6], (DEPTH, DEC_BATCH, ML_HEADS))
    inp['w_ada'] = nrm(ks[7], (DEPTH, D_MODEL, N_MOD * D_MODEL)) * D_MODEL ** -0.5
    inp['b_ada'] = 0.02 * nrm(ks[8], (DEPTH, N_MOD * D_MODEL))
    inp['g_norm1'] = 1.0 + 0.05 * nrm(ks[9], (DEPTH, D_MODEL))
    inp['w_in'] = nrm(ks[10], (DEPTH, D_MODEL, N_IN)) * D_MODEL ** -0.5
    f_bias = jnp.broadcast_to(jnp.linspace(3.0, 6.0, ML_HEADS, dtype=f), (DEPTH, ML_HEADS))
    i_bias = 0.1 * nrm(ks[11], (DEPTH, ML_HEADS))
    inp['b_gate'] = jnp.concatenate([i_bias, f_bias + 0.05 * nrm(ks[12], (DEPTH, ML_HEADS))], axis=-1)
    inp['g_mlstm_head'] = 1.0 + 0.05 * nrm(ks[13], (DEPTH, ML_HEADS, ML_DV))
    inp['ln_v_g'] = 1.0 + 0.05 * nrm(ks[14], (DEPTH, CM_HEADS, CM_HEAD_DIM))
    inp['ln_v_b'] = 0.02 * nrm(ks[15], (DEPTH, CM_HEADS, CM_HEAD_DIM))
    inp['w_s'] = nrm(ks[16], (DEPTH, CM_HEADS, CM_CHUNK, CM_CHUNK)) * CM_CHUNK ** -0.5
    inp['b_s'] = 1.0 + 0.1 * nrm(ks[17], (DEPTH, CM_HEADS, CM_CHUNK))
    inp['w_out'] = nrm(ks[18], (DEPTH, MIX_WIDTH, D_MODEL)) * MIX_WIDTH ** -0.5
    inp['g_norm2'] = 1.0 + 0.05 * nrm(ks[19], (DEPTH, D_MODEL))
    inp['w_gate_up'] = nrm(ks[20], (DEPTH, D_MODEL, 2 * D_FF)) * D_MODEL ** -0.5
    inp['w_down'] = nrm(ks[21], (DEPTH, D_FF, D_MODEL)) * D_FF ** -0.5
    inp['g_final'] = 1.0 + 0.05 * nrm(ks[22], (D_MODEL,))
    return inp

def reference(x_prompt, x_sample, c_prompt, c_sample, state_mlstm_C, state_mlstm_n, state_mlstm_m,
              w_ada, b_ada, g_norm1, w_in, b_gate, g_mlstm_head, ln_v_g, ln_v_b, w_s, b_s,
              w_out, g_norm2, w_gate_up, w_down, g_final):
    f32 = jnp.float32
    xp, xs = x_prompt, x_sample
    Cp_l, np_l, mp_l, Cs_l, ns_l, ms_l, vs_l = [], [], [], [], [], [], []
    for l in range(DEPTH):
        params = (w_ada[l], b_ada[l], g_norm1[l], w_in[l], b_gate[l], g_mlstm_head[l], ln_v_g[l],
                  ln_v_b[l], w_s[l], b_s[l], w_out[l], g_norm2[l], w_gate_up[l], w_down[l])
        C0 = jnp.zeros((BATCH, ML_HEADS, ML_DV, ML_DK), f32)
        n0 = jnp.zeros((BATCH, ML_HEADS, ML_DK), f32)
        m0 = jnp.zeros((BATCH, ML_HEADS), f32)
        xp, Cp, n_p, mp, _ = hybrid_layer(xp, c_prompt, C0, n0, m0, *params)
        xs, Cs, n_s, ms, vs_new = hybrid_layer(xs, c_sample, state_mlstm_C[l], state_mlstm_n[l],
                                               state_mlstm_m[l], *params)
        Cp_l.append(Cp); np_l.append(n_p); mp_l.append(mp)
        Cs_l.append(Cs); ns_l.append(n_s); ms_l.append(ms); vs_l.append(vs_new)
    y_prompt = rmsnorm(xp, g_final)
    y_sample = rmsnorm(xs, g_final)
    return (y_prompt, y_sample,
            jnp.stack(Cp_l), jnp.stack(np_l), jnp.stack(mp_l),
            jnp.stack(Cs_l), jnp.stack(ns_l), jnp.stack(ms_l),
            jnp.stack(vs_l))


_drawn_inputs = setup_inputs


def setup_inputs(seed=0):
    import zlib

    import numpy as np

    out = dict(_drawn_inputs(seed))
    spreads = {}
    factors = {'g_mlstm_head': 4.37, 'ln_v_b': 2.856}
    for name, (base, spread) in spreads.items():
        noise = np.random.default_rng([zlib.crc32(name.encode()), seed]).standard_normal(out[name].shape)
        drawn = base * np.exp(spread * noise) if base else spread * noise
        out[name] = __import__('jax').numpy.asarray(drawn.astype(out[name].dtype))
    for name, factor in factors.items():
        out[name] = (out[name] * factor).astype(out[name].dtype)
    return out
```

```python
from contextlib import ExitStack

import concourse.bass as bass
from concourse import mybir

F32 = mybir.dt.float32
F32R = mybir.dt.float32r
BF16 = mybir.dt.bfloat16
ALU = mybir.AluOpType
ACT = mybir.ActivationFunctionType
AX = mybir.AxisListType

P = 128
D = 1024
KT = D // P
SEQ = 2048
BLK = 512
NBLK = SEQ // BLK
TT = BLK // P
H = 4
HW = H * P
NB = 8
R = NB + 1
NMOD = 6
DFF = 2816
FT = DFF // P
N_IN = 6 * HW + 2 * H
Q0, K0, V0, O0, GATE0 = 0, HW, 2 * HW, 3 * HW, 4 * HW
U0 = GATE0 + 2 * H
S0 = U0 + HW
EPS = 1e-6
QSCALE = float(P) ** -0.5
MASKED = -1.0e30

IN_COLS = [c0 + P * i for c0 in (V0, K0, Q0, S0, O0, U0) for i in range(H)]
N_WIN = len(IN_COLS)
N_OUT = KT
S_OUT = N_WIN
S_UP = S_OUT + N_OUT
S_DOWN = S_UP + 2 * FT
DOWN_K = [(0, 6), (6, 11), (11, 17), (17, 22)]
ND = len(DOWN_K)
NSLAB = S_DOWN + ND * KT

PRE = [0, 1, 2, 3, "R1", 4, "V0", "R2", 5, "V1", "R3", 6, "V2", 7, "R4", "V3", 8, 9, "COL", 10, "WD", 11]
MIX = ["A0", 12, "B0", 13, "A1", 14, "B1", 15, "GV", "A2", 16, "B2", 17, "VST", 18, "A3", 19, "SO", "B3",
       20, "LN", 21, "CMS", "CU0", "CU1", 22, "CU2", "ML", 23, "CU3"]

PR_G1, PR_G2, PR_HEAD, PR_LNG = 0, 8, 16, 20
NPR = 24

DOWN_THIN = [(0, 8), (8, 16), (16, 22)]
UPW = DFF // 8


class Signal:

    def __init__(self, sem, per=0, before=0):
        self.sem, self.per, self.before = sem, per, before

    def at(self, blk, n):
        return blk * self.per + (self.before + n)


def hybrid_step(nc, x_prompt, x_sample, c_prompt, c_sample, state_C, state_n, state_m, w_ada, b_ada,
                g_norm1, w_in, b_gate, g_head, ln_g, ln_b, w_s, b_s, w_out, g_norm2, w_gate_up,
                w_down, g_final, y_prompt, y_sample, C_prompt, n_prompt, m_prompt, C_sample, n_sample,
                m_sample, vs_sample):
    ctx = ExitStack()
    with ctx:
        base = 16512

        def place(name, shape, dt, at):
            return nc.alloc_sbuf_tensor_at(name, shape, dt, offset=base + at)

        top = [0]

        def new(name, shape, dt):
            n = 4 if dt != BF16 else 2
            for s in shape[1:]:
                n *= s
            at = top[0]
            top[0] += (n + 31) // 32 * 32
            return place(name, shape, dt, at), at

        hT_hi, HT = new("hT_hi", [P, KT, BLK], F32R)
        hT_lo, _ = new("hT_lo", [P, KT, BLK], F32R)
        act_hi, U = new("act_hi", [P, FT, BLK], F32R)
        act_lo, _ = new("act_lo", [P, FT, BLK], F32R)
        x_sb, X = new("x_sb", [P, TT, D], F32)
        x1, X1 = new("x1", [P, TT, D], F32)
        work, WK = new("work", [P, 4, BLK], F32)
        raw, _ = new("raw", [P, 2, KT, P], F32)
        w_hi, WH = new("w_hi", [P, 2, KT, P], F32R)
        w_lo, WL = new("w_lo", [P, 2, KT, P], F32R)
        kb = 1024
        qT = place("qT", [P, H, BLK], F32, U)
        kT = place("kT", [P, H, BLK], F32, U + 8 * kb)
        vT = place("vT", [P, H, BLK], F32, U + 16 * kb)
        v_tm = place("v_tm", [P, TT, H, P], F32, U + 24 * kb)
        sigT = place("sigT", [P, H, BLK], F32, U + 32 * kb)
        uT = place("uT", [P, H, BLK], F32, U + 40 * kb)
        vsT = place("vsT", [P, H, BLK], F32, U + 48 * kb)
        mix_hi = place("mix_hi", [P, 2 * H, BLK], F32R, U + 56 * kb)
        mix_lo = place("mix_lo", [P, 2 * H, BLK], F32R, U + 72 * kb)
        rows = place("rows", [P, 8, BLK], F32, U + 32 * kb)
        vs_tm = place("vs_tm", [P, TT, H, P], F32, U + 56 * kb)
        hm = place("hm", [P, TT, H, P], F32, U + 16 * kb)
        E_sb = place("E_sb", [P, H, P], F32, X1)
        P_sb = place("P_sb", [P, H, P], F32, X1 + 2 * kb)
        vg = place("vg", [P, H, P], F32, X1 + 4 * kb)
        k_tm = place("k_tm", [P, H, P], F32, X1 + 6 * kb)
        col = place("col", [P, TT, P], F32, X1 + 8 * kb)
        RT = place("RT", [P, BLK], F32, X1 + 10 * kb)
        R1 = place("R1", [P, BLK], F32, X1 + 12 * kb)
        CT, _ = new("CT", [P, H, P], F32)
        NT, _ = new("NT", [P, H], F32)
        mst, _ = new("mst", [P, TT + 1], F32)
        sel, _ = new("sel", [P, H, P], F32)
        last_row, _ = new("last_row", [P, P], F32)
        wT, _ = new("wT", [P, H, P], F32)
        bias_cm, _ = new("bias_cm", [P, H, P], F32)
        g_fin, _ = new("g_fin", [P, D], F32)
        mask, _ = new("mask", [P, P], BF16)
        identb, _ = new("identb", [P, P], BF16)
        ident, _ = new("ident", [P, P], F32)
        gw_hi, _ = new("gw_hi", [P, KT * 36 + 92], F32R)
        gw_lo, _ = new("gw_lo", [P, KT * 36 + 92], F32R)
        modT, _ = new("modT", [P, NMOD * KT], F32)
        prmT, _ = new("prmT", [P, NPR], F32)
        A1, _ = new("A1", [P, KT], F32)
        A2, _ = new("A2", [P, KT], F32)
        gb, _ = new("gb", [P, 1], F32)
        onecol, _ = new("onecol", [P, 1], F32)
        onerow, _ = new("onerow", [P, P], F32)
        zrow, _ = new("zrow", [H, P], F32)
        half, _ = new("half", [P, 32], F32)
        junk, _ = new("junk", [P, D], BF16)
        dg, _ = new("dg", [P, TT, P], F32)
        ssum, _ = new("ssum", [P, 2, TT], F32)
        ssall, _ = new("ssall", [P, TT], F32)
        msq, _ = new("msq", [P, TT], F32)
        rrt, _ = new("rrt", [P, TT], F32)
        WD, _ = new("WD", [P, TT, H], F32)
        dd, _ = new("dd", [P, 4, H], F32)
        SS, _ = new("SS", [P, TT, H], F32)
        SSm, _ = new("SSm", [P, TT, H], F32)
        rml, _ = new("rml", [P, TT, H], F32)
        bst, _ = new("bst", [P, H, 6], F32)
        MV, _ = new("MV", [P, TT, H, 2], F32)
        lnv, _ = new("lnv", [P, TT, H], F32)
        rln, _ = new("rln", [P, TT, H], F32)
        assert base + top[0] <= 229344, top[0]

        stage = place("stage", [P, 4, KT * 512], F32, U)
        proj = place("proj", [NB, N_IN], F32, U + 64 * kb)
        sact = place("sact", [NB, DFF], F32, U + 77 * kb - 512)
        mod = place("mod", [R, NMOD * D], F32, HT)
        hTs = place("hTs", [P, KT, R], F32, HT + 24 * kb)
        aTs = place("aTs", [P, FT, NB], F32, HT + 25 * kb)
        mixTs = place("mixTs", [P, 2 * H, NB], F32, HT + 26 * kb)
        prm = place("prm", [NPR, P], F32, HT + 27 * kb)
        C0 = place("C0", [P, NB, H, P], F32, X)
        hrow = place("hrow", [NB, D], F32, X1)
        g1b = place("g1b", [NB, D], F32, X1 + 4 * kb)
        sel8 = place("sel8", [NB, NB, P], F32, X1 + 8 * kb)
        lnrow = place("lnrow", [NB, 2, HW], F32, X1 + 12 * kb)
        xs = place("xs", [R, D], F32, WK)
        tmp = place("tmp", [P, D], F32, WK + 4 * kb)
        w_raw = place("w_raw", [P, H, P], F32, WH)
        gw_raw = place("gw_raw", [P, KT * 36 + 92], F32, WH + 2 * kb)
        lnb_lh = place("lnb_lh", [2, H, P], F32, WH + 4 * kb)
        cmb_rh = place("cmb_rh", [2, H, P], F32, WH + 6 * kb)
        n0 = place("n0", [NB, H, P], F32, WL)
        bcx = place("bcx", [NB, 4, H, NB], F32, WL + 2 * kb)
        colq = place("colq", [P, 16, H, NB], F32, WL + 3 * kb)
        g2b = place("g2b", [NB, D], F32, HT + 28 * kb)
        sm = {}
        for n, w in (("g", 8), ("bg", 8), ("nA", 4), ("e", 4), ("l", 4), ("lf", 4), ("mi", 4), ("m", 4),
                     ("m0", 4), ("em", 4), ("qk", 4), ("nq", 4), ("den", 4), ("den2", 4), ("quant", 16),
                     ("ss", 1), ("ms", 1), ("r", 1), ("w00", 4), ("bs0", 4), ("mean", 4), ("var", 4),
                     ("rv", 4)):
            sm[n] = new("s_" + n, [NB, w], F32)[0]
        assert base + top[0] <= 229344, top[0]

        bank = [ctx.enter_context(nc.psum_tensor(f"bank{i}", [P, 512], F32)) for i in range(8)]
        G = bank[0:2]
        T = bank[2:4]
        SP_, EP_, N1, N2 = bank[4:8]

        VST_BANK = [T[0], T[1], N1, N2]
        CMS_BANK = [SP_, EP_, N1, N2]
        NT_BANK = [SP_, EP_, N1, N2]

        sems = {}

        def sem(name):
            if name not in sems:
                sems[name] = ctx.enter_context(nc.semaphore(name))
            return sems[name]

        def signal(name, per, before=0):
            return Signal(sem(name), per, before)

        raw_in = [signal(f"raw_in{i}", 16 * NSLAB // 2) for i in range(2)]
        hi_done = signal("hi_done", NSLAB)
        lo_done = signal("lo_done", NSLAB)
        slab_used = signal("slab_used", NSLAB, 1)
        evac = signal("evac", N_WIN + N_OUT + FT + KT, 1)
        gated = signal("gated", FT, 1)
        act_hi_done = signal("act_hi_done", FT)
        act_ready = signal("act_ready", FT)
        ztr = signal("ztr", 2 * KT, 2)
        zadd = signal("zadd", 2 * KT, 2)
        x_in = signal("x_in", 16)
        x_next = signal("x_next", 1)
        squared = signal("squared", 4 * TT, TT)
        ms = signal("ms", 3, 1)
        rs = signal("rs", 3, 1)
        dg_done = signal("dg_done", 2, 1)
        trx = signal("trx", 2 * KT, KT)
        h32 = signal("h32", 2 * KT, KT)
        h_ready = signal("h_ready", 2 * KT, KT + 2)
        y_done = signal("y_done", 1)
        y_out = signal("y_out", 16)
        x1_free = signal("x1_free", 1)
        gates_ps = signal("gates_ps", 1)
        row_n = signal("row_n", 1)
        row_l = signal("row_l", 1)
        row_m = signal("row_m", 1)
        rt_ready = signal("rt_ready", 1)
        col_ps = signal("col_ps", 1)
        col_done = signal("col_done", 1)
        wd_ps = signal("wd_ps", 1)
        wd_done = signal("wd_done", 1)
        vtr = signal("vtr", TT)
        vtm_done = signal("vtm_done", TT)
        ktr = signal("ktr", TT)
        row_e = signal("row_e", 1)
        a_done = signal("a_done", TT)
        ktm_done = signal("ktm_done", TT)
        e_done = signal("e_done", TT)
        p_ready = signal("p_ready", TT)
        vg_done = signal("vg_done", TT)
        b_done = signal("b_done", TT)
        num_done = signal("num_done", TT)
        den_read = signal("den_read", TT)
        ct_done = signal("ct_done", TT, 1)
        ssm_done = signal("ssm_done", 1)
        rml_done = signal("rml_done", 1)
        vstr = signal("vstr", TT)
        vstm_done = signal("vstm_done", TT)
        lnv_done = signal("lnv_done", 1)
        rln_done = signal("rln_done", 1)
        vn_done = signal("vn_done", 1)
        gv_done = signal("gv_done", 1)
        so_done = signal("so_done", 1)
        cms = signal("cms", H)
        hm_done = signal("hm_done", 1)
        hmtr = signal("hmtr", H)
        mix_read = signal("mix_read", H)
        cms_read = signal("cms_read", H)
        mix_ready = signal("mix_ready", H)
        cu_ready = signal("cu_ready", H)

        block = ctx.enter_context(nc.Block())

        def each_head(ap, n=P):
            return ap.unsqueeze(2).broadcast_to([ap.shape[0], ap.shape[1], n])

        ada_v = w_ada[0].rearrange("(k p) n -> p k n", p=P)
        in_v = w_in[0].rearrange("(k p) n -> p k n", p=P)
        out_v = w_out[0].rearrange("(k p) n -> p k n", p=P)
        up_v = w_gate_up[0].rearrange("(k p) n -> p k n", p=P)
        down_v = w_down[0].rearrange("(k p) n -> p k n", p=P)

        N_ADA = NMOD * D // 512
        thin_in_cols = [(Q0, HW), (K0, HW), (V0, HW), (O0, HW), (U0, HW), (S0, HW), (GATE0, 2 * H)]
        TH_IN = N_ADA
        TH_OUT = TH_IN + len(thin_in_cols)
        TH_UP = TH_OUT + 2
        TH_DOWN = TH_UP + 16
        thin_in = [signal(f"thin_in{i}", 0) for i in range(4)]
        thin_used = signal("thin_used", 0, 4)
        thin_ev = signal("thin_ev", 0, 2)

        def stage_of(t, nk, n):
            return stage[:, t % 4, 0:nk * n].rearrange("p (k n) -> p k n", k=nk)

        @block.sync
        def _(sp):
            sp.dma_start(xs[0:NB, :], c_sample).then_inc(sem("c_in"), 16)
            sp.dma_start(xs[NB:R, :], c_prompt).then_inc(sem("cp_in"), 16)
            sp.dma_start(mod[:, :], b_ada.broadcast_to([R, NMOD * D]))\
                .then_inc(sem("bada_in"), 16)

            def thin_load(t, view, k0, k1, c, n, tt=None):
                sp.wait_ge(thin_used.sem, thin_used.at(0, -3) + (t if tt is None else tt))
                sp.dma_start(stage_of(t, k1 - k0, n), view[:, k0:k1, c]).then_inc(thin_in[t % 4].sem, 16)

            with sp.Fori(0, N_ADA // 4) as i:
                for u in range(4):
                    thin_load(u, ada_v, 0, KT, bass.ds(i * 2048 + u * 512, 512), 512, i * 4 + u)
            for j, (c, n) in enumerate(thin_in_cols):
                thin_load(TH_IN + j, in_v, 0, KT, slice(c, c + n), n)
            for j in range(2):
                thin_load(TH_OUT + j, out_v, 0, KT, slice(512 * j, 512 * j + 512), 512)
            with sp.Fori(0, 4) as i:
                for u in range(4):
                    c = (u // 2) * UPW + (u % 2) * DFF
                    thin_load(TH_UP + u, up_v, 0, KT, bass.ds(i * (2 * UPW) + c, UPW), UPW, i * 4 + TH_UP + u)
            for j in range(2):
                for m, (k0, k1) in enumerate(DOWN_THIN):
                    thin_load(TH_DOWN + 3 * j + m, down_v, k0, k1, slice(512 * j, 512 * j + 512), 512)

            def load(blk, s, src, nk):
                if blk is not None:
                    sp.wait_ge(lo_done.sem, lo_done.at(blk, s - 1))
                sp.dma_start(raw[:, s % 2, 0:nk, :], src).then_inc(raw_in[s % 2].sem, 16)

            def load_in(blk, s):
                c = IN_COLS[s % NSLAB]
                load(blk, s, in_v[:, :, c:c + P], KT)

            load_in(None, 0)
            load_in(None, 1)
            with sp.Fori(0, NBLK) as blk:
                for s in range(2, N_WIN):
                    load_in(blk, s)
                with sp.Fori(0, N_OUT // 2) as i:
                    for u in range(2):
                        sp.wait_ge(lo_done.sem, lo_done.at(blk, S_OUT + u - 1) + i * 2)
                        sp.dma_start(raw[:, u, :, :], out_v[:, :, bass.ds(i * (2 * P) + u * P, P)])\
                            .then_inc(raw_in[u].sem, 16)
                with sp.Fori(0, FT) as i:
                    for u in range(2):
                        sp.wait_ge(lo_done.sem, lo_done.at(blk, S_UP + u - 1) + i * 2)
                        sp.dma_start(raw[:, u, :, :], up_v[:, :, bass.ds(i * P + u * DFF, P)])\
                            .then_inc(raw_in[u].sem, 16)
                with sp.Fori(0, KT) as i:
                    for q, (k0, k1) in enumerate(DOWN_K):
                        sp.wait_ge(lo_done.sem, lo_done.at(blk, S_DOWN + q - 1) + i * ND)
                        sp.dma_start(raw[:, q % 2, 0:k1 - k0, :], down_v[:, k0:k1, bass.ds(i * P, P)])\
                            .then_inc(raw_in[q % 2].sem, 16)
                for s in (NSLAB, NSLAB + 1):
                    load_in(blk, s)
            for i in range(2):
                sp.wait_ge(raw_in[i].sem, raw_in[i].at(NBLK, 16))

        @block.gpsimd
        def _(pool):
            pool.memset(half[:, :], -0.5).then_inc(sem("half_set"), 1)
            pool.memset(ident[:, :], 0.0).then_inc(sem("z_ident"), 1)
            pool.memset(identb[:, :], 0.0).then_inc(sem("z_ident"), 1)
            pool.memset(mask[:, :], 0.0).then_inc(sem("z_ident"), 1)
            pool.memset(last_row[:, :], 0.0).then_inc(sem("z_ident"), 1)
            pool.memset(sel[:, :, :], 0.0).then_inc(sem("z_ident"), 1)
            pool.wait_ge(sem("z_ident"), 5)
            for m in (ident, identb):
                pool.affine_select(out=m[:, :], in_=m[:, :], compare_op=ALU.not_equal, fill=1.0, base=0,
                                   pattern=[[-1, P]], channel_multiplier=1).then_inc(sem("consts"), 1)
            pool.affine_select(out=mask[:, :], in_=mask[:, :], compare_op=ALU.is_ge, fill=MASKED, base=0,
                               pattern=[[1, P]], channel_multiplier=-1).then_inc(sem("consts"), 1)
            pool.affine_select(out=last_row[:, :], in_=last_row[:, :], compare_op=ALU.not_equal, fill=1.0,
                               base=-(P - 1), pattern=[[0, P]], channel_multiplier=1)\
                .then_inc(sem("consts"), 1)
            pool.affine_select(out=sel[:, :, :], in_=sel[:, :, :], compare_op=ALU.not_equal, fill=1.0,
                               base=0, pattern=[[-1, H], [0, P]], channel_multiplier=1)\
                .then_inc(sem("consts"), 1)
            pool.wait_ge(sem("ws_in"), 16)
            pool.affine_select(out=w_raw[:, :, :], in_=w_raw[:, :, :], compare_op=ALU.is_ge, fill=0.0,
                               base=0, pattern=[[0, H], [-1, P]], channel_multiplier=1)\
                .then_inc(sem("ws_masked"), 1)

            def power(done, out, src, width, rows):
                pool.tensor_tensor(out, src, half[0:rows, 0:width], ALU.pow).then_inc(done, 1)

            pool.wait_ge(sem("half_set"), 1)
            pool.wait_ge(sem("ms1s"), 1)
            power(sem("r1s"), sm["r"][:, :], sm["ms"][:, :], 1, NB)
            pool.wait_ge(sem("msml"), 1)
            power(sem("rmls"), colq[:, 9].rearrange("p h b -> p (h b)"),
                  colq[:, 8].rearrange("p h b -> p (h b)"), H * NB, P)
            pool.wait_ge(sem("vars"), 1)
            power(sem("rvs"), sm["rv"][:, :], sm["var"][:, :], H, NB)
            pool.wait_ge(sem("ms2s"), 1)
            power(sem("r2s"), sm["r"][:, :], sm["ms"][:, :], 1, NB)
            pool.wait_ge(sem("ms3s"), 1)
            power(sem("r3s"), sm["r"][:, :], sm["ms"][:, :], 1, NB)

            x_v = x_prompt[0].rearrange("(b i p) d -> b p i d", p=P, i=TT)
            y_v = y_prompt[0].rearrange("(b i p) d -> b p i d", p=P, i=TT)
            pool.wait_ge(sem("thin_out"), 80)
            pool.dma_start(x_sb[:, :, :], x_v[0]).then_inc(x_in.sem, 16)

            def root(blk, n):
                pool.wait_ge(ms.sem, ms.at(blk, n + 1))
                power(rs.sem, rrt[:, :], msq[:, :], TT, P)

            def pool_block(blk, last):
                for c in range(TT):
                    if c == 0:
                        pool.wait_ge(col_done.sem, col_done.at(blk, 1))
                    else:
                        pool.wait_ge(b_done.sem, b_done.at(blk, c))
                    pool.wait_ge(vtm_done.sem, vtm_done.at(blk, c + 1))
                    wg = each_head(col[:, c, 96:96 + H])
                    pool.tensor_tensor(vg[:, :, :], v_tm[:, c], wg, ALU.mult).then_inc(vg_done.sem, 1)
                    if c == 2:
                        pool.wait_ge(lnv_done.sem, lnv_done.at(blk, 1))
                        power(rln_done.sem, rln[:, :, :].rearrange("p c h -> p (c h)"),
                              lnv[:, :, :].rearrange("p c h -> p (c h)"), TT * H, P)
                pool.wait_ge(ssm_done.sem, ssm_done.at(blk, 1))
                power(rml_done.sem, rml[:, :, :].rearrange("p c h -> p (c h)"),
                      SSm[:, :, :].rearrange("p c h -> p (c h)"), TT * H, P)
                root(blk, 0)
                if not last:
                    pool.wait_ge(zadd.sem, zadd.at(blk, KT))
                    pool.dma_start(x_sb[:, :, :], x_v[bass.ds(blk + 1, 1)].rearrange("o p i d -> p (o i) d"))\
                        .then_inc(x_in.sem, 16)
                    pool.wait_ge(x_in.sem, x_in.at(blk, 32))
                pool.sem_inc(x_next.sem, 1)
                root(blk, 1)
                root(blk, 2)
                pool.wait_ge(y_done.sem, y_done.at(blk, 1))
                pool.dma_start(y_v[bass.ds(blk, 1)].rearrange("o p i d -> p (o i) d"), x1[:, :, :])\
                    .then_inc(y_out.sem, 16)
                pool.wait_ge(y_out.sem, y_out.at(blk, 16))
                if not last:
                    pool.sem_inc(x1_free.sem, 1)

            root(0, -1)
            pool.sem_inc(x1_free.sem, 1)
            with pool.Fori(0, NBLK - 1) as blk:
                pool_block(blk, False)
            pool_block(NBLK - 1, True)

            pool.dma_start(m_prompt[0].rearrange("o h -> h o"), mst[0:H, 0:1]).then_inc(sem("fin_out"), 16)
            pool.wait_ge(sem("fin_set"), 1)
            pool.dma_start(C_prompt[0, 0].rearrange("h e d -> e h d"),
                           work[:, 0].rearrange("p (h d) -> p h d", h=H)).then_inc(sem("fin_out"), 16)
            pool.dma_start(n_prompt[0, 0], work[0:H, 1, 0:P]).then_inc(sem("fin_out"), 16)
            pool.wait_ge(sem("fin_out"), 48)

        @block.scalar
        def _(act):
            def fetch(name, dst, src, single=False):
                act.dma_start(dst, src, allow_slow_non_contiguous=single).then_inc(sem(name), 16)

            fetch("prm_in", prm[PR_G1:PR_G1 + KT, :], g_norm1[0].rearrange("(k p) -> k p", p=P))
            fetch("prm_in", prm[PR_G2:PR_G2 + KT, :], g_norm2[0].rearrange("(k p) -> k p", p=P))
            fetch("prm_in", prm[PR_HEAD:PR_HEAD + H, :], g_head[0])
            fetch("prm_in", prm[PR_LNG:PR_LNG + H, :], ln_g[0])
            fetch("ws_in", w_raw[:, :, :], w_s[0].rearrange("h t s -> t h s"))
            act.wait_ge(sem("lh_one"), 1)
            fetch("cmb_in", lnb_lh[0:1, :, :], ln_b)
            fetch("cmb_in", cmb_rh[1:2, :, :], b_s)
            act.wait_ge(sem("gw_zero"), 1)
            gcols = gw_raw[:, 0:KT * 36].rearrange("p (k c) -> p k c", c=36)
            fetch("gw_in", gcols[:, :, 0:H], in_v[:, :, GATE0:GATE0 + H])
            fetch("gw_in", gcols[:, :, 32:32 + H], in_v[:, :, GATE0 + H:GATE0 + 2 * H])
            act.wait_ge(sem("gb_zero"), 1)
            fetch("gb_in", gb[0:H, :], b_gate[0, 0:H].rearrange("(h o) -> h o", o=1))
            fetch("gb_in", gb[32:32 + H, :], b_gate[0, H:2 * H].rearrange("(h o) -> h o", o=1))
            act.wait_ge(sem("c_in"), 16)
            act.wait_ge(sem("cp_in"), 16)
            act.activation(xs[:, :], xs[:, :], ACT.Silu).then_inc(sem("c_silu"), 1)
            fetch("srow_in", g1b[:, :], g_norm1.broadcast_to([NB, D]))
            fetch("srow_in", g2b[:, :], g_norm2.broadcast_to([NB, D]))
            fetch("srow_in", lnrow[:, 0, :], ln_g.rearrange("o h e -> o (h e)").broadcast_to([NB, HW]))
            fetch("srow_in", lnrow[:, 1, :], ln_b.rearrange("o h e -> o (h e)").broadcast_to([NB, HW]))
            fetch("srow_in", sm["bg"][:, :], b_gate.broadcast_to([NB, 2 * H]))
            fetch("srow_in", sm["m0"][:, :], state_m[0])
            fetch("srow_in", n0[:, :, :], state_n[0])
            fetch("srow_in", sm["w00"][:, :], w_s[:, :, 0, 0].broadcast_to([NB, H]), True)
            fetch("srow_in", sm["bs0"][:, :], b_s[:, :, 0].broadcast_to([NB, H]), True)
            fetch("C_in", C0[:, :, :, :], state_C[0].rearrange("b h e d -> e b h d"))
            fetch("gf_in", g_fin[:, :], g_final.rearrange("(o d) -> o d", o=1).broadcast_to([P, D]))

            act.wait_ge(sem("cT_ps"), 1)
            fetch("xs_in", xs[0:NB, :], x_sample.rearrange("b s d -> (b s) d"))

            def sample_squares(done):
                act.activation(tmp[0:NB, :], xs[0:NB, :], ACT.Square, accum_out=sm["ss"][:, :])\
                    .then_inc(done, 1)

            act.wait_ge(sem("xs_in"), 16)
            sample_squares(sem("ss1s"))
            act.wait_ge(sem("nAs"), 1)
            act.activation(sm["e"][:, :], sm["nA"][:, :], ACT.Exp).then_inc(sem("es"), 1)
            act.wait_ge(sem("es"), 1)
            act.activation(sm["l"][:, :], sm["e"][:, :], ACT.Ln, bias=1.0).then_inc(sem("ls"), 1)
            act.wait_ge(sem("wargs"), 1)
            act.activation(sm["quant"][:, 4:12], sm["quant"][:, 4:12], ACT.Exp).then_inc(sem("wexp"), 1)
            act.activation(sm["em"][:, :], sm["m"][:, :], ACT.Exp, scale=-1.0).then_inc(sem("wexp"), 1)
            fetch("thin_out", m_sample[0], sm["m"][:, :])
            act.activation(proj[:, U0:U0 + 2 * HW], proj[:, U0:U0 + 2 * HW], ACT.Gelu_apprx_tanh)\
                .then_inc(sem("gelus"), 1)
            act.wait_ge(sem("oTs"), 1)
            act.activation(colq[:, 10], colq[:, 1], ACT.Sigmoid).then_inc(sem("sigs"), 1)
            act.wait_ge(sem("n_new"), 1)
            fetch("thin_out", n_sample[0], n0[:, :, :])
            act.wait_ge(sem("C_upd"), NB)
            fetch("thin_out", C_sample[0].rearrange("b h e d -> e b h d"), C0[:, :, :, :])
            act.wait_ge(sem("vs_new"), 1)
            fetch("thin_out", vs_sample[0].rearrange("b s h e -> (b s) (h e)"), proj[:, S0:S0 + HW])
            act.wait_ge(sem("x1s"), 2)
            sample_squares(sem("ss2s"))
            with act.Fori(0, 4) as i:
                for u in range(2):
                    act.wait_ge(thin_used.sem, thin_used.at(0, TH_UP + 2 * u + 1) + i * 4)
                    act.wait_ge(sem("sacts"), 1 + u + i * 2)
                    act.activation(tmp[0:NB, 512 * u:512 * u + UPW], G[(TH_UP + 2 * u) % 2][0:NB, 0:UPW],
                                   ACT.Silu).then_inc(sem("silus"), 1)
            act.wait_ge(sem("x2s"), 2)
            sample_squares(sem("ss3s"))
            act.wait_ge(sem("y_s"), 1)
            fetch("thin_out", y_sample.rearrange("b s d -> (b s) d"), hrow[:, :])
            act.wait_ge(sem("thin_out"), 80)

            def split_hi(blk, s, used=True, j=0):
                act.wait_ge(raw_in[s % 2].sem, raw_in[s % 2].at(blk, 16 * (s // 2 + 1)) + j * 8)
                if used:
                    act.wait_ge(slab_used.sem, slab_used.at(blk, s - 1) + j)
                act.activation(w_hi[:, s % 2], raw[:, s % 2], ACT.Copy).then_inc(hi_done.sem, 1)

            def squares(blk, n, x_tiles, c0=0, c1=D, part=0):
                if n >= 0:
                    act.wait_ge(ms.sem, ms.at(blk, n))
                before = {-1: -TT, 0: part * TT, 1: 2 * TT, 2: 3 * TT}[n]
                for i in range(TT):
                    if n >= 0 or i > 0:
                        act.wait_ge(squared.sem, squared.at(blk, before + i))
                    act.activation(junk[:, c0:c1], x_tiles[:, i, c0:c1], ACT.Square,
                                   accum_out=ssum[:, part, i:i + 1]).then_inc(squared.sem, 1)

            def norm_tile(blk, n, k, a_col, b_col):
                act.wait_ge(trx.sem, trx.at(blk, n * KT + k + 1))
                act.wait_ge(h_ready.sem, h_ready.at(blk, n * KT + k - 1))
                act.activation(work[:, 2 + k % 2], NT_BANK[k % 4][:, :], ACT.Identity,
                               scale=a_col[:, k:k + 1], bias=b_col[:, k:k + 1]).then_inc(h32.sem, 1)

            def mix_slab(blk, s):
                h = s % H
                dst, f, scale = [(vT, ACT.Copy, 1.0), (kT, ACT.Copy, 1.0), (qT, ACT.Copy, QSCALE),
                                 (vsT, ACT.Copy, 1.0), (sigT, ACT.Copy, 1.0),
                                 (uT, ACT.Gelu_apprx_tanh, 1.0)][s // H]
                act.wait_ge(slab_used.sem, slab_used.at(blk, s + 1))
                act.activation(dst[:, h, :], G[s % 2][:, :], f, scale=scale).then_inc(evac.sem, 1)

            def gate_log(blk):
                act.wait_ge(row_n.sem, row_n.at(blk, 1))
                act.activation(rows[0:H, 3, :], rows[0:H, 2, :], ACT.Exp).then_inc(row_e.sem, 1)
                act.wait_ge(row_e.sem, row_e.at(blk, 1))
                act.activation(rows[0:H, 4, :], rows[0:H, 3, :], ACT.Ln, bias=1.0).then_inc(row_l.sem, 1)

            def gate_weights(blk):
                act.wait_ge(row_m.sem, row_m.at(blk, 1))
                for c in range(TT):
                    t = slice(c * P, (c + 1) * P)
                    act.activation(RT[32:32 + H, t], rows[0:H, 6, t], ACT.Exp, scale=-1.0,
                                   bias=mst[0:H, c:c + 1])
                    act.activation(RT[96:96 + H, t], RT[0:H, t], ACT.Exp,
                                   bias=R1[0:H, (c + 1) * P - 1:(c + 1) * P])
                act.activation(RT[64:64 + H, :], rows[0:H, 7, :], ACT.Exp, scale=-1.0)\
                    .then_inc(rt_ready.sem, 1)

            def chunk_a(blk, c):
                act.wait_ge(ktr.sem, ktr.at(blk, c + 1))
                if c > 0:
                    act.wait_ge(b_done.sem, b_done.at(blk, c))
                act.activation(k_tm[:, :, :], T[0][:, :], ACT.Copy).then_inc(ktm_done.sem, 1)
                act.wait_ge(a_done.sem, a_done.at(blk, c + 1))
                if c > 0:
                    act.wait_ge(p_ready.sem, p_ready.at(blk, c))
                for h in range(H):
                    ins = act.activation(E_sb[:, h, :], EP_[:, h * P:(h + 1) * P], ACT.Exp,
                                         bias=col[:, c, h:h + 1])
                ins.then_inc(e_done.sem, 1)

            def act_block(blk):
                for step in PRE + MIX:
                    if isinstance(step, int):
                        if step > 0:
                            split_hi(blk, step + 1)
                        mix_slab(blk, step)
                    elif step == "GV":
                        act.wait_ge(evac.sem, evac.at(blk, 4 * H))
                        act.activation(vsT[:, :, :], vsT[:, :, :], ACT.Gelu_apprx_tanh)\
                            .then_inc(gv_done.sem, 1)
                    elif step == "SO":
                        act.wait_ge(evac.sem, evac.at(blk, 5 * H))
                        act.activation(sigT[:, :, :], sigT[:, :, :], ACT.Sigmoid).then_inc(so_done.sem, 1)
                    elif step == "R2":
                        gate_log(blk)
                    elif step == "R4":
                        gate_weights(blk)
                    elif step[:-1] == "V":
                        c = int(step[1])
                        act.wait_ge(vtr.sem, vtr.at(blk, c + 1))
                        act.activation(v_tm[:, c], T[c % 2][:, :], ACT.Copy).then_inc(vtm_done.sem, 1)
                    elif step[:-1] == "A":
                        chunk_a(blk, int(step[1]))
                with act.Fori(0, N_OUT // 2 - 1) as i:
                    for u in range(2):
                        split_hi(blk, S_OUT + u + 1, j=i * 2)
                        out_gate(blk, i, u, S_OUT + u + 1, 2, 0, modT, 2 * KT)
                split_hi(blk, S_OUT + 7)
                out_gate(blk, 3, 0, S_OUT + 1, 2, 0, modT, 2 * KT)
                split_hi(blk, S_OUT + 8)
                act.wait_ge(zadd.sem, zadd.at(blk, KT - 2))
                squares(blk, 0, x1, 0, D - 2 * P, 0)
                out_gate(blk, 3, 1, S_OUT + 2, 2, 0, modT, 2 * KT)
                act.wait_ge(zadd.sem, zadd.at(blk, KT))
                squares(blk, 0, x1, D - 2 * P, D, 1)
                for k in range(KT):
                    norm_tile(blk, 0, k, A2, modT[:, 3 * KT:4 * KT])
                with act.Fori(0, FT) as i:
                    split_hi(blk, S_UP + 1, j=i * 2)
                    act.wait_ge(slab_used.sem, slab_used.at(blk, S_UP + 1) + i * 2)
                    act.wait_ge(gated.sem, gated.at(blk, 0) + i)
                    act.activation(work[:, 2], G[0][:, :], ACT.Silu).then_inc(evac.sem, 1)
                    split_hi(blk, S_UP + 2, j=i * 2)
                    act.wait_ge(gated.sem, gated.at(blk, 1) + i)
                    act.activation(act_hi[:, bass.ds(i, 1), :], work[:, 3:4, :], ACT.Copy)\
                        .then_inc(act_hi_done.sem, 1)
                act.wait_ge(x_next.sem, x_next.at(blk, 1))
                squares(blk, 1, x_sb)

                def split_four(n, j=0):
                    for q in range(ND):
                        split_hi(blk, S_DOWN + ND * n + q + 1, j=j)

                def next_tiles(ks):
                    for k in ks:
                        norm_tile(blk, 1, k, A1, modT[:, 0:KT])

                split_four(0)
                next_tiles(range(4))
                out_gate(blk, 0, 0, S_DOWN + ND, 2 * ND, KT, modT, 5 * KT)
                with act.Fori(0, 3) as i:
                    split_four(1, i * (2 * ND))
                    out_gate(blk, i, 1, S_DOWN + 2 * ND, 2 * ND, KT, modT, 5 * KT)
                    split_four(2, i * (2 * ND))
                    out_gate(blk, i, 2, S_DOWN + 3 * ND, 2 * ND, KT, modT, 5 * KT)
                split_four(7)
                next_tiles(range(4, 8))
                out_gate(blk, 3, 1, S_DOWN + 2 * ND, 2 * ND, KT, modT, 5 * KT)
                split_hi(blk, NSLAB + 1)
                act.wait_ge(zadd.sem, zadd.at(blk, 2 * KT))
                squares(blk, 2, x1)

            def out_gate(blk, i, u, done, step, first, gates, g0):
                act.wait_ge(slab_used.sem, slab_used.at(blk, done) + i * step)
                act.wait_ge(ztr.sem, ztr.at(blk, first + u - 1) + i * 2)
                act.activation(work[:, u % 2], G[u % 2][:, :], ACT.Copy,
                               scale=gates[:, bass.ds(i * 2 + (g0 + u), 1)]).then_inc(evac.sem, 1)

            split_hi(0, 0, used=False)
            split_hi(0, 1, used=False)
            act.wait_ge(x_in.sem, 16)
            squares(0, -1, x_sb)
            for k in range(KT):
                norm_tile(0, -1, k, A1, modT[:, 0:KT])
            with act.Fori(0, NBLK) as blk:
                act_block(blk)

        @block.vector
        def _(ve):
            TH_CHAIN, BLK_CHAIN = 200, 400
            chain = signal("ve_chain", BLK_CHAIN, TH_CHAIN)
            at = {"blk": None, "n": 0}

            def link(ins):
                at["n"] += 1
                ins.then_inc(chain.sem, 1)
                if at["blk"] is None:
                    ve.wait_ge(chain.sem, at["n"])
                else:
                    ve.wait_ge(chain.sem, chain.at(at["blk"], at["n"]))

            def round_off(n):
                while at["n"] < n:
                    k = min(n - at["n"], 100)
                    ve.sem_inc(chain.sem, k)
                    at["n"] += k
                assert at["n"] == n, at["n"]

            ve.memset(lnb_lh[:, :, :], 1.0).then_inc(sem("lh_one"), 1)
            ve.memset(gw_raw[:, :], 0.0).then_inc(sem("gw_zero"), 1)
            ve.memset(gb[:, :], 0.0).then_inc(sem("gb_zero"), 1)
            ve.memset(onecol[:, :], 1.0)
            ve.memset(onerow[:, :], 1.0).then_inc(sem("ones"), 1)
            ve.memset(zrow[:, :], 0.0)
            ve.memset(CT[:, :, :], 0.0)
            ve.memset(NT[:, :], 0.0)
            link(ve.memset(mst[:, :], 0.0))
            ve.wait_ge(sem("consts"), 5)
            ve.tensor_copy(sel8[:, :, :], each_head(ident[0:NB, 0:NB])).then_inc(sem("sel8_set"), 1)
            ve.wait_ge(sem("prm_ps"), 1)
            link(ve.tensor_copy(prmT[:, :], T[1][:, 0:NPR]))
            ve.wait_ge(sem("gb_in"), 32)
            ve.wait_ge(sem("gw_in"), 32)
            link(ve.tensor_copy(gw_hi[:, :], gw_raw[:, :]))
            ve.tensor_tensor(gw_lo[:, :], gw_raw[:, :], gw_hi[:, :].bitcast(F32), ALU.subtract)
            ve.wait_ge(sem("wT_ps"), 1)
            ve.tensor_copy(wT[:, :, :], N1[:, :]).then_inc(sem("wT_set"), 1)
            ve.wait_ge(sem("rsum_ps"), 1)
            ve.tensor_copy(cmb_rh[0:1, :, :], N2[0:1, :]).then_inc(sem("rsum_set"), 1)
            ve.wait_ge(sem("bcm_ps"), 1)
            ve.tensor_copy(bias_cm[:, :, :], EP_[:, :]).then_inc(sem("bcm_set"), 1)
            ve.wait_ge(sem("cT_ps"), 1)
            ve.tensor_copy(hTs[:, :, :], T[0][:, 0:KT * R]).then_inc(sem("cT_set"), 1)

            ve.wait_ge(sem("bada_in"), 16)
            with ve.Fori(0, N_ADA // 2) as i:
                for u in range(2):
                    ve.wait_ge(thin_used.sem, thin_used.at(0, u + 1) + i * 2)
                    m = mod[:, bass.ds(i * 1024 + u * 512, 512)]
                    ve.tensor_tensor(m, G[u][0:R, :], m, ALU.add).then_inc(thin_ev.sem, 1)
            ve.wait_ge(sem("modT_ps"), 1)
            link(ve.tensor_copy(modT[:, :],
                                SP_[:, 0:NMOD * KT * R].rearrange("p (j r) -> p j r", r=R)[:, :, NB]))
            ve.scalar_tensor_tensor(out=A1[:, :], in0=modT[:, KT:2 * KT], scalar=1.0,
                                    in1=prmT[:, PR_G1:PR_G1 + KT], op0=ALU.add, op1=ALU.mult)
            ve.scalar_tensor_tensor(out=A2[:, :], in0=modT[:, 4 * KT:5 * KT], scalar=1.0,
                                    in1=prmT[:, PR_G2:PR_G2 + KT], op0=ALU.add, op1=ALU.mult)

            def sample_norm(sums, mean, root, gain):
                ve.wait_ge(sem(sums), 1)
                ve.tensor_scalar(sm["ms"][:, :], sm["ss"][:, :], 1.0 / D, EPS, ALU.mult, ALU.add)\
                    .then_inc(sem(mean), 1)
                ve.wait_ge(sem(root), 1)
                ve.wait_ge(sem("srow_in"), 144)
                return ve.scalar_tensor_tensor(out=hrow[:, :], in0=xs[0:NB, :], scalar=sm["r"][:, :],
                                               in1=gain, op0=ALU.mult, op1=ALU.mult)

            def modulate(shift, scale, done):
                link(ve.scalar_tensor_tensor(out=tmp[0:NB, :], in0=mod[0:NB, scale * D:(scale + 1) * D],
                                             scalar=1.0, in1=hrow[:, :], op0=ALU.add, op1=ALU.mult))
                ve.tensor_tensor(hrow[:, :], tmp[0:NB, :], mod[0:NB, shift * D:(shift + 1) * D], ALU.add)\
                    .then_inc(sem(done), 1)

            def sample_columns(ps_ready, done):
                ve.wait_ge(sem(ps_ready), 1)
                ve.tensor_copy(hTs[:, :, 0:NB], T[1][:, 0:KT * NB].rearrange("p (k b) -> p k b", b=NB))\
                    .then_inc(sem(done), 1)

            def residual(first, gate, slabs, done):
                for j in range(2):
                    c = slice(512 * j, 512 * j + 512)
                    ve.wait_ge(thin_used.sem, thin_used.at(0, slabs[j]))
                    link(ve.tensor_tensor(tmp[0:NB, c], G[(first + j) % 2][0:NB, :],
                                          mod[0:NB, gate * D + 512 * j:gate * D + 512 * j + 512], ALU.mult))
                    thin_ev_ins = ve.tensor_tensor(xs[0:NB, c], xs[0:NB, c], tmp[0:NB, c], ALU.add)
                    thin_ev_ins.then_inc(sem(done), 1)

            link(sample_norm("ss1s", "ms1s", "r1s", g1b[:, :]))
            modulate(0, 1, "h1s")
            sample_columns("h1T_ps", "h1T_set")
            for j, (c, n) in enumerate(thin_in_cols):
                ve.wait_ge(thin_used.sem, thin_used.at(0, TH_IN + j + 1))
                link(ve.tensor_copy(proj[:, c:c + n], G[(TH_IN + j) % 2][0:NB, 0:n]))
                ve.sem_inc(thin_ev.sem, 1)
            q8, k8, v8 = (proj[:, c:c + HW] for c in (Q0, K0, V0))
            by_head = lambda a: a.rearrange("b (h e) -> b h e", h=H)
            wi8, wg8, s8, rd8 = (sm["quant"][:, 4 * i:4 * i + 4] for i in (1, 2, 0, 3))
            g = sm["g"]
            ve.tensor_copy(sm["den"][:, :], sm["m0"][:, :]).then_inc(sem("proj_set"), 1)
            link(ve.tensor_tensor(g[:, :], proj[:, GATE0:GATE0 + 2 * H], sm["bg"][:, :], ALU.add))
            ve.scalar_tensor_tensor(out=sm["nA"][:, :], in0=g[:, H:2 * H], scalar=-1.0, in1=g[:, H:2 * H],
                                    op0=ALU.mult, op1=ALU.min).then_inc(sem("nAs"), 1)
            ve.wait_ge(sem("ls"), 1)
            link(ve.scalar_tensor_tensor(out=sm["lf"][:, :], in0=g[:, H:2 * H], scalar=0.0,
                                         in1=sm["l"][:, :], op0=ALU.min, op1=ALU.subtract))
            link(ve.tensor_tensor(sm["mi"][:, :], sm["lf"][:, :], sm["m0"][:, :], ALU.add))
            link(ve.tensor_tensor(sm["m"][:, :], sm["mi"][:, :], g[:, 0:H], ALU.max))
            ve.tensor_tensor(wi8, sm["mi"][:, :], sm["m"][:, :], ALU.subtract)
            ve.tensor_tensor(wg8, g[:, 0:H], sm["m"][:, :], ALU.subtract).then_inc(sem("wargs"), 1)
            link(ve.tensor_tensor(tmp[0:NB, 0:HW], q8, k8, ALU.mult))
            ve.tensor_reduce(sm["qk"][:, :], by_head(tmp[0:NB, 0:HW]), AX.X, ALU.add)
            link(ve.tensor_tensor(tmp[0:NB, HW:2 * HW], n0[:, :, :].rearrange("b h e -> b (h e)"), q8,
                                  ALU.mult))
            link(ve.tensor_reduce(sm["nq"][:, :], by_head(tmp[0:NB, HW:2 * HW]), AX.X, ALU.add))
            ve.wait_ge(sem("wexp"), 2)
            ve.scalar_tensor_tensor(out=s8, in0=sm["qk"][:, :], scalar=QSCALE, in1=wg8, op0=ALU.mult,
                                    op1=ALU.mult)
            link(ve.scalar_tensor_tensor(out=sm["den"][:, :], in0=sm["nq"][:, :], scalar=QSCALE, in1=wi8,
                                         op0=ALU.mult, op1=ALU.mult))
            link(ve.tensor_tensor(sm["den2"][:, :], sm["den"][:, :], s8, ALU.add))
            link(ve.scalar_tensor_tensor(out=sm["den"][:, :], in0=sm["den2"][:, :], scalar=-1.0,
                                         in1=sm["den2"][:, :], op0=ALU.mult, op1=ALU.max))
            link(ve.tensor_tensor(sm["den2"][:, :], sm["den"][:, :], sm["em"][:, :], ALU.max))
            link(ve.reciprocal(rd8, sm["den2"][:, :]))
            ve.tensor_tensor(n0[:, :, :], n0[:, :, :], each_head(wi8), ALU.mult)
            link(ve.tensor_tensor(by_head(tmp[0:NB, 0:HW]), by_head(k8), each_head(wg8), ALU.mult))
            ve.tensor_tensor(n0[:, :, :], n0[:, :, :], by_head(tmp[0:NB, 0:HW]), ALU.add)\
                .then_inc(sem("n_new"), 1)
            for i in range(4):
                ins = ve.tensor_tensor(bcx[:, i, :, :],
                                       ident[0:NB, 0:NB].unsqueeze(1).broadcast_to([NB, H, NB]),
                                       sm["quant"][:, 4 * i:4 * i + 4].unsqueeze(2)
                                       .broadcast_to([NB, H, NB]), ALU.mult)
            ins.then_inc(sem("bcx_set"), 1)
            ve.wait_ge(sem("bc_ps"), 1)
            ve.tensor_copy(colq[:, 12:16, :, :].rearrange("p a h b -> p (a h b)"), EP_[:, 0:4 * H * NB])
            ve.wait_ge(sem("vo_ps"), 1)
            ve.tensor_copy(colq[:, 0:2, :, :].rearrange("p a h b -> p (a h b)"), N2[:, 0:2 * H * NB])\
                .then_inc(sem("oTs"), 1)
            link(ve.tensor_copy(sm["ms"][:, :], sm["ss"][:, :]))
            sT, wiT, wgT, rdT = (colq[:, 12 + i] for i in range(4))
            link(ve.tensor_tensor(colq[:, 3], colq[:, 0], wgT, ALU.mult))
            ve.wait_ge(sem("C_in"), 16)
            for b in range(NB):
                ve.wait_ge(sem("qkb"), b + 1)
                Qb = T[b % 2][:, :].rearrange("p (h d) -> p h d", h=H)
                Kb = bank[4 + b % 2][:, :].rearrange("p (h d) -> p h d", h=H)
                t0 = tmp[:, 0:HW].rearrange("p (h d) -> p h d", h=H)
                t1 = tmp[:, HW:2 * HW].rearrange("p (h d) -> p h d", h=H)
                link(ve.tensor_tensor(t0, C0[:, b], Qb, ALU.mult))
                ve.tensor_reduce(colq[:, 2, :, b], t0, AX.X, ALU.add)
                ve.tensor_tensor(C0[:, b], C0[:, b], each_head(wiT[:, :, b]), ALU.mult)
                link(ve.tensor_tensor(t1, Kb, each_head(colq[:, 3, :, b]), ALU.mult))
                ve.tensor_tensor(C0[:, b], C0[:, b], t1, ALU.add).then_inc(sem("C_upd"), 1)
            ve.wait_ge(sem("C_upd"), NB)
            ve.tensor_tensor(colq[:, 4], colq[:, 0], sT, ALU.mult)
            link(ve.scalar_tensor_tensor(out=colq[:, 5], in0=colq[:, 2], scalar=QSCALE, in1=wiT,
                                         op0=ALU.mult, op1=ALU.mult))
            link(ve.tensor_tensor(colq[:, 6], colq[:, 4], colq[:, 5], ALU.add))
            link(ve.tensor_tensor(colq[:, 11], colq[:, 6], rdT, ALU.mult))
            ve.tensor_tensor(colq[:, 7], colq[:, 11], colq[:, 11], ALU.mult).then_inc(sem("sqml"), 1)
            ve.wait_ge(sem("ssml_ps"), 1)
            ve.tensor_scalar(colq[:, 8].rearrange("p h b -> p (h b)"), N1[:, 0:H * NB], 1.0 / P, EPS,
                             ALU.mult, ALU.add).then_inc(sem("msml"), 1)
            vs8, u8 = proj[:, S0:S0 + HW], proj[:, U0:U0 + HW]
            ta, tb = tmp[0:NB, 0:HW], tmp[0:NB, HW:2 * HW]
            ve.wait_ge(sem("gelus"), 1)
            link(ve.tensor_reduce(sm["mean"][:, :], by_head(vs8), AX.X, ALU.add))
            link(ve.tensor_scalar(sm["den"][:, :], sm["mean"][:, :], 1.0 / P, None, ALU.mult))
            link(ve.tensor_tensor(by_head(vs8), by_head(vs8), each_head(sm["den"][:, :]), ALU.subtract))
            link(ve.tensor_tensor(ta, vs8, vs8, ALU.mult))
            link(ve.tensor_reduce(sm["mean"][:, :], by_head(ta), AX.X, ALU.add))
            ve.tensor_scalar(sm["var"][:, :], sm["mean"][:, :], 1.0 / P, EPS, ALU.mult, ALU.add)\
                .then_inc(sem("vars"), 1)
            ve.wait_ge(sem("rmls"), 1)
            ve.wait_ge(sem("sigs"), 1)
            link(ve.tensor_tensor(colq[:, 6], colq[:, 11], colq[:, 9], ALU.mult))
            for h in range(H):
                ve.scalar_tensor_tensor(out=mixTs[:, h, :], in0=colq[:, 6, h, :],
                                        scalar=prmT[:, PR_HEAD + h:PR_HEAD + h + 1],
                                        in1=colq[:, 10, h, :], op0=ALU.mult, op1=ALU.mult)
            ve.wait_ge(sem("rvs"), 1)
            link(ve.tensor_tensor(by_head(vs8), by_head(vs8), each_head(sm["rv"][:, :]), ALU.mult))
            link(ve.tensor_tensor(vs8, vs8, lnrow[:, 0, :], ALU.mult))
            link(ve.tensor_tensor(vs8, vs8, lnrow[:, 1, :], ALU.add))
            ve.sem_inc(sem("vs_new"), 1)
            link(ve.tensor_tensor(by_head(ta), by_head(vs8), each_head(sm["w00"][:, :]), ALU.mult))
            link(ve.tensor_tensor(by_head(tb), by_head(ta), each_head(sm["bs0"][:, :]), ALU.add))
            ve.tensor_tensor(ta, tb, u8, ALU.mult).then_inc(sem("hcm"), 1)
            ve.wait_ge(sem("hcm_ps"), 1)
            ve.tensor_copy(mixTs[:, H:2 * H, :].rearrange("p h b -> p (h b)"), T[0][:, 0:H * NB])\
                .then_inc(sem("mixs"), 1)
            residual(TH_OUT, 2, [TH_OUT + 1, TH_OUT + 2], "x1s")
            link(sample_norm("ss2s", "ms2s", "r2s", g2b[:, :]))
            modulate(3, 4, "h2s")
            sample_columns("h2T_ps", "h2T_set")
            ve.sem_inc(sem("sacts"), 1)
            ve.sem_inc(thin_ev.sem, 2)
            with ve.Fori(0, 4) as i:
                for u in range(2):
                    ve.wait_ge(thin_used.sem, thin_used.at(0, TH_UP + 2 * u + 2) + i * 4)
                    ve.wait_ge(sem("silus"), i * 2 + (u + 1))
                    link_u = ve.tensor_tensor(sact[:, bass.ds(i * (2 * UPW) + u * UPW, UPW)],
                                              tmp[0:NB, 512 * u:512 * u + UPW],
                                              G[(TH_UP + 2 * u + 1) % 2][0:NB, 0:UPW], ALU.mult)
                    link_u.then_inc(sem("sacts"), 1)
            ve.wait_ge(sem("aT_ps"), 1)
            ve.tensor_copy(aTs[:, :, :].rearrange("p f b -> p (f b)"), T[0][:, 0:FT * NB])\
                .then_inc(sem("aT_set"), 1)
            residual(37, 5, [TH_DOWN + 3, TH_DOWN + 6], "x2s")
            sample_norm("ss3s", "ms3s", "r3s", g_fin[0:NB, :]).then_inc(sem("y_s"), 1)
            ve.wait_ge(sem("thin_out"), 80)

            def split_lo(blk, s, j=0):
                ve.wait_ge(hi_done.sem, hi_done.at(blk, s + 1) + j)
                ve.tensor_tensor(w_lo[:, s % 2], raw[:, s % 2], w_hi[:, s % 2].bitcast(F32),
                                 ALU.subtract).then_inc(lo_done.sem, 1)

            def split_vector(dst_hi, dst_lo, src):
                link(ve.tensor_copy(dst_hi, src))
                return ve.tensor_tensor(dst_lo, src, dst_hi.bitcast(F32), ALU.subtract)

            def mean_square(blk, n):
                ve.wait_ge(squared.sem, squared.at(blk, {-1: 0, 0: 2 * TT, 1: 3 * TT, 2: 4 * TT}[n]))
                sums = ssum[:, 0, :]
                if n == 0:
                    link(ve.tensor_tensor(ssall[:, :], ssum[:, 0, :], ssum[:, 1, :], ALU.add))
                    sums = ssall[:, :]
                ve.tensor_scalar(msq[:, :], sums, 1.0 / D, EPS, ALU.mult, ALU.add).then_inc(ms.sem, 1)
                ve.wait_ge(rs.sem, rs.at(blk, n + 1))

            def diagonals(blk, n):
                mean_square(blk, n)
                ve.tensor_tensor(dg[:, :, :], ident[:, :].unsqueeze(1).broadcast_to([P, TT, P]),
                                 each_head(rrt[:, :]), ALU.mult).then_inc(dg_done.sem, 1)

            def norm_tiles(blk, n, ks):
                for k in ks:
                    ve.wait_ge(h32.sem, h32.at(blk, n * KT + k + 1))
                    split_vector(hT_hi[:, k, :], hT_lo[:, k, :], work[:, 2 + k % 2])\
                        .then_inc(h_ready.sem, 1)

            def gate_sum(blk):
                rI, rF, rN = (rows[0:H, i, :] for i in range(3))
                ve.wait_ge(x1_free.sem, x1_free.at(blk, 1))
                ve.memset(R1[:, :], 0.0)
                ve.memset(RT[:, :], 0.0)
                ve.wait_ge(gates_ps.sem, gates_ps.at(blk, 1))
                ve.tensor_scalar(rI, EP_[0:H, :], gb[0:H, :], None, ALU.add)
                link(ve.tensor_scalar(rF, EP_[32:32 + H, :], gb[32:32 + H, :], None, ALU.add))
                ve.scalar_tensor_tensor(out=rN, in0=rF, scalar=-1.0, in1=rF, op0=ALU.mult, op1=ALU.min)\
                    .then_inc(row_n.sem, 1)

            def gate_scans(blk):
                rI, rF, rlf, rL, rb, rM, rbm = (rows[0:H, i, :] for i in (0, 1, 2, 4, 5, 6, 7))
                ve.wait_ge(row_l.sem, row_l.at(blk, 1))
                link(ve.scalar_tensor_tensor(out=rlf, in0=rF, scalar=0.0, in1=rL, op0=ALU.min,
                                             op1=ALU.subtract))
                for c in range(TT):
                    t = slice(c * P, (c + 1) * P)
                    ins = ve.tensor_tensor_scan(rows[0:H, 5, t], onerow[0:H, :], rows[0:H, 2, t], 0.0,
                                                ALU.mult, ALU.add)
                link(ins)
                link(ve.tensor_tensor(RT[0:H, :], rI, rb, ALU.subtract))
                for c in range(TT):
                    t = slice(c * P, (c + 1) * P)
                    last = (c + 1) * P - 1
                    link(ve.tensor_tensor_scan(rows[0:H, 6, t], zrow[:, :], RT[0:H, t], mst[0:H, c:c + 1],
                                               ALU.add, ALU.max))
                    link(ve.tensor_tensor(mst[0:H, c + 1:c + 2], rows[0:H, 5, last:last + 1],
                                          rows[0:H, 6, last:last + 1], ALU.add))
                ve.tensor_scalar(R1[0:H, :], rM, -1.0, None, ALU.mult)
                ve.tensor_tensor(rbm, rb, rM, ALU.add).then_inc(row_m.sem, 1)

            def gate_columns(blk):
                ve.wait_ge(col_ps.sem, col_ps.at(blk, 1))
                ve.tensor_copy(col[:, :, :], SP_[:, :]).then_inc(col_done.sem, 1)
                link(ve.tensor_copy(mst[0:H, 0:1], mst[0:H, TT:TT + 1]))

            def decays(blk):
                ve.wait_ge(wd_ps.sem, wd_ps.at(blk, 1))
                link(ve.tensor_copy(WD[:, :, :].rearrange("p c h -> p (c h)"), T[1][:, 0:TT * H]))
                ve.sem_inc(wd_done.sem, 1)

            heads = lambda ps: ps[:, :].rearrange("p (h e) -> p h e", h=H)

            def chunk_a(blk, c):
                ve.wait_ge(a_done.sem, a_done.at(blk, c + 1))
                ve.wait_ge(e_done.sem, e_done.at(blk, c + 1))
                ve.tensor_tensor(P_sb[:, :, :], E_sb[:, :, :], heads(SP_), ALU.mult).then_inc(p_ready.sem, 1)

            def chunk_b(blk, c):
                wi = col[:, c, 32:32 + H]
                em = col[:, c, 64:64 + H]
                ve.wait_ge(b_done.sem, b_done.at(blk, c + 1))
                ve.tensor_tensor(CT[:, :, :], CT[:, :, :], each_head(WD[:, c, :]), ALU.mult)
                link(ve.tensor_tensor(NT[:, :], NT[:, :], WD[:, c, :], ALU.mult))
                ve.tensor_tensor(CT[:, :, :], CT[:, :, :], heads(T[0]), ALU.add)
                ve.tensor_tensor(NT[:, :], NT[:, :], T[1][:, 0:H], ALU.add).then_inc(ct_done.sem, 1)
                w2 = work[:, 2].rearrange("p (h e) -> p h e", h=H)
                w3 = work[:, 3].rearrange("p (h e) -> p h e", h=H)
                ve.tensor_tensor(w2, heads(N2), each_head(wi), ALU.mult)
                link(ve.tensor_tensor(dd[:, 0, :], EP_[:, H:2 * H], wi, ALU.mult))
                ve.tensor_tensor(hm[:, c], w2, heads(N1), ALU.add).then_inc(num_done.sem, 1)
                link(ve.tensor_tensor(dd[:, 1, :], dd[:, 0, :], EP_[:, 0:H], ALU.add))
                ve.sem_inc(den_read.sem, 1)
                link(ve.scalar_tensor_tensor(out=dd[:, 2, :], in0=dd[:, 1, :], scalar=-1.0,
                                             in1=dd[:, 1, :], op0=ALU.mult, op1=ALU.max))
                link(ve.tensor_tensor(dd[:, 3, :], dd[:, 2, :], em, ALU.max))
                link(ve.reciprocal(dd[:, 0, :], dd[:, 3, :]))
                link(ve.tensor_tensor(hm[:, c], hm[:, c], each_head(dd[:, 0, :]), ALU.mult))
                link(ve.tensor_tensor(w3, hm[:, c], hm[:, c], ALU.mult))
                link(ve.tensor_reduce(SS[:, c, :], w3, AX.X, ALU.add))
                if c == TT - 1:
                    ve.tensor_scalar(SSm[:, :, :], SS[:, :, :], 1.0 / P, EPS, ALU.mult, ALU.add)\
                        .then_inc(ssm_done.sem, 1)

            def vs_stats(blk):
                for c in range(TT):
                    ve.wait_ge(vstr.sem, vstr.at(blk, c + 1))
                    for h in range(H):
                        ve.bn_stats(bst[:, h, :], VST_BANK[c][:, h * P:(h + 1) * P])
                    link(ve.tensor_copy(vs_tm[:, c], heads(VST_BANK[c])))
                    ve.sem_inc(vstm_done.sem, 1)
                    for h in range(H):
                        ins = ve.bn_aggr(MV[:, c, h, :], bst[:, h, :])
                    link(ins)
                ve.tensor_scalar(lnv[:, :, :], MV[:, :, :, 1], EPS, None, ALU.add).then_inc(lnv_done.sem, 1)

            def vs_norm(blk):
                v = vs_tm[:, :, :, :].rearrange("p c h e -> p (c h) e")
                mean = MV[:, :, :, 0].rearrange("p c h -> p (c h)")
                link(ve.tensor_tensor(v, v, each_head(mean), ALU.subtract))
                ve.wait_ge(rln_done.sem, rln_done.at(blk, 1))
                ve.tensor_tensor(v, v, each_head(rln[:, :, :].rearrange("p c h -> p (c h)")), ALU.mult)\
                    .then_inc(vn_done.sem, 1)

            def spatial(blk):
                for h in range(H):
                    ve.wait_ge(cms.sem, cms.at(blk, h + 1))
                    out = vsT[:, h, :].rearrange("p (c t) -> p c t", c=TT)
                    ve.scalar_tensor_tensor(out=out, in0=heads(CMS_BANK[h]),
                                            scalar=prmT[:, PR_LNG + h:PR_LNG + h + 1],
                                            in1=bias_cm[:, h, :].unsqueeze(1).broadcast_to([P, TT, P]),
                                            op0=ALU.mult, op1=ALU.add).then_inc(cms_read.sem, 1)

            def gate_u(blk, h):
                ve.wait_ge(evac.sem, evac.at(blk, 5 * H + h + 1))
                ve.wait_ge(cms_read.sem, cms_read.at(blk, h + 1))
                link(ve.tensor_tensor(work[:, h % 2], vsT[:, h, :], uT[:, h, :], ALU.mult))
                split_vector(mix_hi[:, H + h, :], mix_lo[:, H + h, :], work[:, h % 2])\
                    .then_inc(cu_ready.sem, 1)

            def finish_heads(blk):
                ve.wait_ge(rml_done.sem, rml_done.at(blk, 1))
                v = hm[:, :, :, :].rearrange("p c h e -> p (c h) e")
                ve.tensor_tensor(v, v, each_head(rml[:, :, :].rearrange("p c h -> p (c h)")), ALU.mult)\
                    .then_inc(hm_done.sem, 1)
                ve.wait_ge(so_done.sem, so_done.at(blk, 1))
                for h in range(H):
                    ve.wait_ge(hmtr.sem, hmtr.at(blk, h + 1))
                    link(ve.scalar_tensor_tensor(out=work[:, 2 + h % 2], in0=T[h % 2][:, :],
                                                 scalar=prmT[:, PR_HEAD + h:PR_HEAD + h + 1],
                                                 in1=sigT[:, h, :], op0=ALU.mult, op1=ALU.mult))
                    ve.sem_inc(mix_read.sem, 1)
                    split_vector(mix_hi[:, h, :], mix_lo[:, h, :], work[:, 2 + h % 2])\
                        .then_inc(mix_ready.sem, 1)

            def add(blk, ev, src, u, c, j=0):
                ve.wait_ge(ztr.sem, ztr.at(blk, ev + 1) + j)
                cols = bass.ds(c, P) if not isinstance(c, int) else slice(c, c + P)
                ve.tensor_tensor(x1[:, :, cols], src[:, :, cols], heads(T[u]), ALU.add)\
                    .then_inc(zadd.sem, 1)

            def output(blk, first, slab0, per, src, tiles=None):
                for q in range(per):
                    split_lo(blk, slab0 + q + 1)
                if tiles is not None:
                    tiles(range(4))
                with ve.Fori(0, 3) as i:
                    for q in range(per):
                        split_lo(blk, slab0 + per + q + 1, j=i * (2 * per))
                    add(blk, first, src, 0, i * (2 * P), j=i * 2)
                    for q in range(per):
                        split_lo(blk, slab0 + 2 * per + q + 1, j=i * (2 * per))
                    add(blk, first + 1, src, 1, i * (2 * P) + P, j=i * 2)
                for q in range(per):
                    split_lo(blk, slab0 + 7 * per + q + 1)
                if tiles is not None:
                    tiles(range(4, 8))
                add(blk, first + 6, src, 0, 6 * P)
                add(blk, first + 7, src, 1, 7 * P)

            handlers = {"R1": gate_sum, "R3": gate_scans, "COL": gate_columns, "WD": decays,
                        "VST": vs_stats, "LN": vs_norm, "CMS": spatial, "ML": finish_heads}

            split_lo(0, 0)
            split_lo(0, 1)
            diagonals(0, -1)
            norm_tiles(0, -1, range(KT))
            round_off(TH_CHAIN)
            with ve.Fori(0, NBLK) as blk:
                at["blk"], at["n"] = blk, 0
                for step in PRE + MIX:
                    if isinstance(step, int):
                        if step > 0:
                            split_lo(blk, step + 1)
                    elif step in handlers:
                        handlers[step](blk)
                    elif step[0] == "A":
                        chunk_a(blk, int(step[1]))
                    elif step[0] == "B":
                        chunk_b(blk, int(step[1]))
                    elif step[:-1] == "CU":
                        gate_u(blk, int(step[2]))
                output(blk, 0, S_OUT, 1, x_sb)
                diagonals(blk, 0)
                norm_tiles(blk, 0, range(KT))
                with ve.Fori(0, FT) as i:
                    for u in range(2):
                        split_lo(blk, S_UP + u + 1, j=i * 2)
                    ve.wait_ge(slab_used.sem, slab_used.at(blk, S_UP + 2) + i * 2)
                    ve.wait_ge(evac.sem, evac.at(blk, N_WIN + N_OUT + 1) + i)
                    ve.tensor_tensor(work[:, 3], work[:, 2], G[1][:, :], ALU.mult).then_inc(gated.sem, 1)
                    ve.wait_ge(act_hi_done.sem, act_hi_done.at(blk, 1) + i)
                    ve.tensor_tensor(act_lo[:, bass.ds(i, 1), :], work[:, 3:4, :],
                                     act_hi[:, bass.ds(i, 1), :].bitcast(F32), ALU.subtract)\
                        .then_inc(act_ready.sem, 1)
                diagonals(blk, 1)
                ve.wait_ge(slab_used.sem, slab_used.at(blk, S_DOWN))
                output(blk, KT, S_DOWN, ND, x1, lambda ks: norm_tiles(blk, 1, ks))
                split_lo(blk, NSLAB + 1)
                mean_square(blk, 2)
                for i in range(TT):
                    ins = ve.scalar_tensor_tensor(out=x1[:, i, :], in0=x1[:, i, :], scalar=rrt[:, i:i + 1],
                                                  in1=g_fin[:, :], op0=ALU.mult, op1=ALU.mult)
                ins.then_inc(y_done.sem, 1)
                round_off(BLK_CHAIN)
            ve.wait_ge(sem("fin_ps"), 1)
            ve.tensor_copy(work[:, 0], T[0][:, :])
            ve.tensor_copy(work[0:H, 1, 0:P], T[1][0:H, 0:P]).then_inc(sem("fin_set"), 1)

        @block.tensor
        def _(pe):
            mm = pe.matmul
            pe.sem_inc(thin_used.sem, 4)
            pe.wait_ge(sem("consts"), 5)
            pe.wait_ge(sem("prm_in"), 64)
            pe.transpose(T[1][:, 0:NPR], prm[:, :], ident[0:NPR, 0:NPR]).then_inc(sem("prm_ps"), 1)
            pe.wait_ge(sem("ws_masked"), 1)
            for h in range(H):
                ins = pe.transpose(N1[:, h * P:(h + 1) * P], w_raw[:, h, :], ident[:, :])
            ins.then_inc(sem("wT_ps"), 1)
            pe.wait_ge(sem("wT_set"), 1)
            pe.wait_ge(sem("ones"), 1)
            mm(N2[0:1, :], onecol[:, :], wT[:, :, :].rearrange("s h t -> s (h t)"), start=True, stop=True)\
                .then_inc(sem("rsum_ps"), 1)
            pe.wait_ge(sem("rsum_set"), 1)
            pe.wait_ge(sem("cmb_in"), 32)
            for h in range(H):
                ins = mm(EP_[:, h * P:(h + 1) * P], lnb_lh[:, h, :], cmb_rh[:, h, :], start=True, stop=True)
            ins.then_inc(sem("bcm_ps"), 1)

            pe.wait_ge(sem("c_silu"), 1)
            for k in range(KT):
                ins = pe.transpose(T[0][:, k * R:(k + 1) * R], xs[:, k * P:(k + 1) * P], ident[0:R, 0:R])
            ins.then_inc(sem("cT_ps"), 1)
            pe.wait_ge(sem("cT_set"), 1)

            def thin(t, out, lhs, k0, k1, n, start=True, stop=True, j=None):
                pe.wait_ge(thin_in[t % 4].sem, 16 * (t // 4 + 1) + (0 if j is None else j * 16))
                st = stage_of(t, k1 - k0, n)
                for k in range(k0, k1):
                    ins = mm(out, lhs[:, k, :], st[:, k - k0, :], start=start and k == k0,
                             stop=stop and k == k1 - 1)
                ins.then_inc(thin_used.sem, 1)

            pe.sem_inc(thin_ev.sem, 2)
            with pe.Fori(0, N_ADA // 4) as i:
                for u in range(4):
                    pe.wait_ge(thin_ev.sem, thin_ev.at(0, u - 1) + i * 4)
                    thin(u, G[u % 2][0:R, :], hTs, 0, KT, 512, j=i)
            pe.wait_ge(thin_ev.sem, thin_ev.at(0, N_ADA))
            for j in range(NMOD * KT):
                ins = pe.transpose(SP_[:, j * R:(j + 1) * R], mod[:, j * P:(j + 1) * P], ident[0:R, 0:R])
            ins.then_inc(sem("modT_ps"), 1)

            def row_columns(row_ready, done):
                pe.wait_ge(sem(row_ready), 1)
                for k in range(KT):
                    ins = pe.transpose(T[1][:, k * NB:(k + 1) * NB], hrow[:, k * P:(k + 1) * P],
                                       ident[0:NB, 0:NB])
                ins.then_inc(sem(done), 1)

            row_columns("h1s", "h1T_ps")
            pe.wait_ge(sem("h1T_set"), 1)
            for j, (c, n) in enumerate(thin_in_cols):
                t = TH_IN + j
                pe.wait_ge(thin_ev.sem, thin_ev.at(0, t - 1))
                thin(t, G[t % 2][0:NB, 0:n], hTs[:, :, 0:NB], 0, KT, n)
            pe.wait_ge(sem("proj_set"), 1)
            for i, c0 in enumerate((V0, O0)):
                for h in range(H):
                    ins = pe.transpose(N2[:, (i * H + h) * NB:(i * H + h + 1) * NB],
                                       proj[:, c0 + h * P:c0 + (h + 1) * P], ident[0:NB, 0:NB])
            ins.then_inc(sem("vo_ps"), 1)
            pe.wait_ge(sem("bcx_set"), 1)
            mm(EP_[:, 0:4 * H * NB], onerow[0:NB, :], bcx[:, :, :, :].rearrange("p a h b -> p (a h b)"),
               start=True, stop=True).then_inc(sem("bc_ps"), 1)
            pe.wait_ge(sem("oTs"), 1)
            pe.wait_ge(sem("sel8_set"), 1)
            for b in range(NB):
                if b >= 2:
                    pe.wait_ge(sem("C_upd"), b - 1)
                mm(T[b % 2][:, :], sel8[:, b, :], proj[:, Q0:Q0 + HW], start=True, stop=True)
                mm(bank[4 + b % 2][:, :], sel8[:, b, :], proj[:, K0:K0 + HW], start=True, stop=True)\
                    .then_inc(sem("qkb"), 1)
            pe.wait_ge(sem("sqml"), 1)
            mm(N1[:, 0:H * NB], onerow[:, :], colq[:, 7].rearrange("p h b -> p (h b)"), start=True,
               stop=True).then_inc(sem("ssml_ps"), 1)
            pe.wait_ge(sem("hcm"), 1)
            for h in range(H):
                ins = pe.transpose(T[0][:, h * NB:(h + 1) * NB], tmp[0:NB, h * P:(h + 1) * P],
                                   ident[0:NB, 0:NB])
            ins.then_inc(sem("hcm_ps"), 1)
            pe.wait_ge(sem("mixs"), 1)
            for j in range(2):
                thin(TH_OUT + j, G[(TH_OUT + j) % 2][0:NB, :], mixTs, 0, KT, 512)
            row_columns("h2s", "h2T_ps")
            pe.wait_ge(sem("h2T_set"), 1)
            with pe.Fori(0, 4) as i:
                for u in range(4):
                    t = TH_UP + u
                    pe.wait_ge(sem("sacts"), i * 2 + (1 + u // 2))
                    thin(t, G[t % 2][0:NB, 0:UPW], hTs[:, :, 0:NB], 0, KT, UPW, j=i)
            pe.wait_ge(sem("sacts"), 9)
            for f in range(FT):
                ins = pe.transpose(T[0][:, f * NB:(f + 1) * NB], sact[:, f * P:(f + 1) * P],
                                   ident[0:NB, 0:NB])
            ins.then_inc(sem("aT_ps"), 1)
            pe.wait_ge(sem("aT_set"), 1)
            for j in range(2):
                for m, (k0, k1) in enumerate(DOWN_THIN):
                    thin(TH_DOWN + 3 * j + m, G[(37 + j) % 2][0:NB, :], aTs, k0, k1, 512, start=m == 0,
                         stop=m == len(DOWN_THIN) - 1)
            pe.wait_ge(sem("thin_out"), 80)

            pe.sem_inc(slab_used.sem, 1)
            pe.sem_inc(ztr.sem, 2)

            def product(out, slot, rhs_hi, rhs_lo, tiles, start=True, stop=True, before_tile=None):
                for n, (k, r) in enumerate(tiles):
                    if before_tile is not None:
                        before_tile(k)
                    last = n == len(tiles) - 1
                    mm(out, w_lo[:, slot, k, :], rhs_hi[:, r, :], start=start and n == 0, stop=False)
                    mm(out, w_hi[:, slot, k, :], rhs_lo[:, r, :], start=False, stop=False)
                    ins = mm(out, w_hi[:, slot, k, :], rhs_hi[:, r, :], start=False, stop=stop and last)
                return ins

            every = [(k, k) for k in range(KT)]

            def slab_ready(blk, s, j=0):
                pe.wait_ge(lo_done.sem, lo_done.at(blk, s + 1) + j)

            def norm_out(blk, n, x_tiles, ks):
                pe.wait_ge(dg_done.sem, dg_done.at(blk, n + 1))
                for k in ks:
                    if k >= 4:
                        pe.wait_ge(h32.sem, h32.at(blk, n * KT + k - 3))
                    for i in range(TT):
                        ins = mm(NT_BANK[k % 4][:, i * P:(i + 1) * P], x_tiles[:, i, k * P:(k + 1) * P],
                                 dg[:, i, :], start=True, stop=True)
                    ins.then_inc(trx.sem, 1)

            def gates(blk):
                pe.wait_ge(h32.sem, h32.at(blk, 0))
                for k in range(KT):
                    w = slice(36 * k, 36 * k + P)
                    pe.wait_ge(h_ready.sem, h_ready.at(blk, k + 1 - KT))
                    mm(EP_[:, :], gw_lo[:, w], hT_hi[:, k, :], start=k == 0, stop=False)
                    mm(EP_[:, :], gw_hi[:, w], hT_lo[:, k, :], start=False, stop=False)
                    ins = mm(EP_[:, :], gw_hi[:, w], hT_hi[:, k, :], start=False, stop=k == KT - 1)
                ins.then_inc(gates_ps.sem, 1)

            def columns(blk):
                pe.wait_ge(rt_ready.sem, rt_ready.at(blk, 1))
                for c in range(TT):
                    ins = pe.transpose(SP_[:, c * P:(c + 1) * P], RT[:, c * P:(c + 1) * P], ident[:, :])
                ins.then_inc(col_ps.sem, 1)

            def decays(blk):
                pe.wait_ge(col_done.sem, col_done.at(blk, 1))
                pe.wait_ge(vtm_done.sem, vtm_done.at(blk, TT))
                mm(T[1][:, 0:TT * H], last_row[:, :], col[:, :, 32:32 + H], start=True, stop=True)\
                    .then_inc(wd_ps.sem, 1)

            def by_tokens(done, src, c, out):
                for h in range(H):
                    ins = pe.transpose(out[:, h * P:(h + 1) * P], src[:, h, c * P:(c + 1) * P],
                                       ident[:, :])
                ins.then_inc(done.sem, 1)

            def v_tokens(blk, c):
                if c == 0:
                    pe.wait_ge(evac.sem, evac.at(blk, H))
                if c >= 2:
                    pe.wait_ge(vtm_done.sem, vtm_done.at(blk, c - 1))
                by_tokens(vtr, vT, c, T[c % 2])

            def chunk_a(blk, c):
                t = slice(c * P, (c + 1) * P)
                if c == 0:
                    pe.wait_ge(evac.sem, evac.at(blk, 3 * H))
                    pe.wait_ge(wd_done.sem, wd_done.at(blk, 1))
                else:
                    pe.wait_ge(ct_done.sem, ct_done.at(blk, c))
                    pe.wait_ge(den_read.sem, den_read.at(blk, c))
                    pe.wait_ge(p_ready.sem, p_ready.at(blk, c))
                if c == 3:
                    pe.wait_ge(vstm_done.sem, vstm_done.at(blk, 1))
                by_tokens(ktr, kT, c, T[0])
                mm(EP_[:, :], identb[:, :], mask[:, :].unsqueeze(1).broadcast_to([P, H, P]), start=True,
                   stop=False)
                for h in range(H):
                    mm(EP_[:, h * P:(h + 1) * P], sel[:, h, :], R1[:, t], start=False, stop=h == H - 1)
                for h in range(H):
                    ins = mm(SP_[:, h * P:(h + 1) * P], kT[:, h, t], qT[:, h, t], start=True, stop=True)
                ins.then_inc(a_done.sem, 1)

            def chunk_b(blk, c):
                t = slice(c * P, (c + 1) * P)
                if c > 0:
                    pe.wait_ge(num_done.sem, num_done.at(blk, c))
                pe.wait_ge(p_ready.sem, p_ready.at(blk, c + 1))
                if c == 3:
                    pe.wait_ge(vstm_done.sem, vstm_done.at(blk, TT))
                for h in range(H):
                    mm(N1[:, h * P:(h + 1) * P], P_sb[:, h, :], v_tm[:, c, h, :], start=True, stop=True)
                    mm(EP_[:, h:h + 1], P_sb[:, h, :], onecol[:, :], start=True, stop=True)
                pe.wait_ge(ct_done.sem, ct_done.at(blk, c))
                for h in range(H):
                    mm(N2[:, h * P:(h + 1) * P], qT[:, h, t], CT[:, h, :], start=True, stop=True)
                    mm(EP_[:, H + h:H + h + 1], qT[:, h, t], NT[:, h:h + 1], start=True, stop=True)
                pe.wait_ge(vg_done.sem, vg_done.at(blk, c + 1))
                pe.wait_ge(ktm_done.sem, ktm_done.at(blk, c + 1))
                for h in range(H):
                    mm(T[0][:, h * P:(h + 1) * P], k_tm[:, h, :], vg[:, h, :], start=True, stop=True)
                    ins = mm(T[1][:, h:h + 1], k_tm[:, h, :], col[:, c, 96 + h:97 + h], start=True,
                             stop=True)
                ins.then_inc(b_done.sem, 1)

            def vs_tokens(blk):
                pe.wait_ge(gv_done.sem, gv_done.at(blk, 1))
                pe.wait_ge(ct_done.sem, ct_done.at(blk, 3))
                pe.wait_ge(num_done.sem, num_done.at(blk, 3))
                for c in range(TT):
                    by_tokens(vstr, vsT, c, VST_BANK[c])

            def spatial(blk):
                pe.wait_ge(vn_done.sem, vn_done.at(blk, 1))
                pe.wait_ge(num_done.sem, num_done.at(blk, TT))
                pe.wait_ge(den_read.sem, den_read.at(blk, TT))
                for h in range(H):
                    for c in range(TT):
                        ins = mm(CMS_BANK[h][:, c * P:(c + 1) * P], vs_tm[:, c, h, :], wT[:, h, :],
                                 start=True, stop=True)
                    ins.then_inc(cms.sem, 1)

            def finish_heads(blk):
                pe.wait_ge(hm_done.sem, hm_done.at(blk, 1))
                pe.wait_ge(ct_done.sem, ct_done.at(blk, TT))
                for h in range(H):
                    if h >= 2:
                        pe.wait_ge(mix_read.sem, mix_read.at(blk, h - 1))
                    for c in range(TT):
                        ins = pe.transpose(T[h % 2][:, c * P:(c + 1) * P], hm[:, c, h, :], ident[:, :])
                    ins.then_inc(hmtr.sem, 1)

            def mix_slab(blk, s):
                slab_ready(blk, s)
                pe.wait_ge(evac.sem, evac.at(blk, max(s - 1, 0)))
                product(G[s % 2][:, :], s % 2, hT_hi, hT_lo, every).then_inc(slab_used.sem, 1)

            def to_tokens(blk, ev, u, n_ev, j=0):
                pe.wait_ge(evac.sem, evac.at(blk, n_ev) + j)
                pe.wait_ge(zadd.sem, zadd.at(blk, ev - 1) + j)
                for i in range(TT):
                    ins = pe.transpose(T[u][:, i * P:(i + 1) * P], work[:, u, i * P:(i + 1) * P],
                                       ident[:, :])
                ins.then_inc(ztr.sem, 1)

            def output(blk, first, e0, gemm, tiles=None):
                gemm(0, 0, 0)
                if tiles is not None:
                    tiles(range(4))
                with pe.Fori(0, 3) as i:
                    gemm(1, 1, i)
                    to_tokens(blk, first, 0, e0 + 1, j=i * 2)
                    gemm(2, 0, i)
                    to_tokens(blk, first + 1, 1, e0 + 2, j=i * 2)
                gemm(7, 1, 0)
                if tiles is not None:
                    tiles(range(4, 8))
                to_tokens(blk, first + 6, 0, e0 + 7)
                to_tokens(blk, first + 7, 1, e0 + 8)

            pe.sem_inc(zadd.sem, 2)
            pe.sem_inc(h_ready.sem, 2)
            pe.sem_inc(evac.sem, 1)
            pe.sem_inc(gated.sem, 1)
            pe.sem_inc(ct_done.sem, 1)
            handlers = {"R1": gates, "COL": columns, "WD": decays, "VST": vs_tokens, "CMS": spatial,
                        "ML": finish_heads}
            norm_out(0, -1, x_sb, range(KT))
            with pe.Fori(0, NBLK) as blk:
                gates(blk)
                for step in PRE + MIX:
                    if isinstance(step, int):
                        mix_slab(blk, step)
                    elif step in ("COL", "WD", "VST", "CMS", "ML"):
                        handlers[step](blk)
                    elif step[0] == "V":
                        v_tokens(blk, int(step[1]))
                    elif step[0] == "A":
                        chunk_a(blk, int(step[1]))
                    elif step[0] == "B":
                        chunk_b(blk, int(step[1]))

                def out_gemm(n, u, i):
                    slab_ready(blk, S_OUT + n, i * 2)
                    pe.wait_ge(evac.sem, evac.at(blk, S_OUT + n - 1) + i * 2)
                    ready = None
                    if n == 0:
                        def ready(k):
                            done = mix_ready if k < H else cu_ready
                            pe.wait_ge(done.sem, done.at(blk, k % H + 1))
                    product(G[u][:, :], u, mix_hi, mix_lo, every, before_tile=ready)\
                        .then_inc(slab_used.sem, 1)

                output(blk, 0, N_WIN, out_gemm)
                norm_out(blk, 0, x1, range(KT))
                with pe.Fori(0, FT) as i:
                    slab_ready(blk, S_UP, i * 2)
                    pe.wait_ge(evac.sem, evac.at(blk, N_WIN + N_OUT) + i)
                    product(G[0][:, :], 0, hT_hi, hT_lo, every,
                            before_tile=lambda k: pe.wait_ge(h_ready.sem, h_ready.at(blk, k + 1)))\
                        .then_inc(slab_used.sem, 1)
                    slab_ready(blk, S_UP + 1, i * 2)
                    pe.wait_ge(gated.sem, gated.at(blk, 0) + i)
                    product(G[1][:, :], 1, hT_hi, hT_lo, every).then_inc(slab_used.sem, 1)
                pe.wait_ge(act_ready.sem, act_ready.at(blk, FT))

                def down_gemm(n, u, i):
                    pe.wait_ge(evac.sem, evac.at(blk, N_WIN + N_OUT + FT + n - 1) + i * 2)
                    for q, (k0, k1) in enumerate(DOWN_K):
                        slab_ready(blk, S_DOWN + ND * n + q, i * (2 * ND))
                        product(G[u][:, :], q % 2, act_hi, act_lo, [(k - k0, k) for k in range(k0, k1)],
                                start=q == 0, stop=q == ND - 1).then_inc(slab_used.sem, 1)

                output(blk, KT, N_WIN + N_OUT + FT, down_gemm,
                       lambda ks: norm_out(blk, 1, x_sb, ks))
            pe.wait_ge(zadd.sem, zadd.at(NBLK - 1, 2 * KT))
            for h in range(H):
                pe.transpose(T[0][:, h * P:(h + 1) * P], CT[:, h, :], ident[:, :])
            pe.transpose(T[1][0:H, 0:P], NT[:, :], ident[:, :]).then_inc(sem("fin_ps"), 1)


_INS = ["x_prompt", "x_sample", "c_prompt", "c_sample", "state_mlstm_C", "state_mlstm_n", "state_mlstm_m",
        "w_ada", "b_ada", "g_norm1", "w_in", "b_gate", "g_mlstm_head", "ln_v_g", "ln_v_b", "w_s", "b_s",
        "w_out", "g_norm2", "w_gate_up", "w_down", "g_final"]
_OUTS = [(1, SEQ, D), (NB, 1, D), (1, 1, H, P, P), (1, 1, H, P), (1, 1, H), (1, NB, H, P, P),
         (1, NB, H, P), (1, NB, H), (1, NB, 1, H, P)]


def kernel(**inputs):
    import numpy as _np
    import concourse.bacc as _bacc
    from concourse import mybir as _mybir
    from concourse.bass_utils import run_bass_kernel_spmd as _run

    nc = _bacc.Bacc("TRN2", target_bir_lowering=False, num_devices=1)
    arrays, args = {}, []
    for name in _INS:
        a = _np.ascontiguousarray(inputs[name])
        arrays[f"in_{name}_dram"] = a
        args.append(nc.dram_tensor(f"in_{name}_dram", a.shape, _mybir.dt.from_np(a.dtype),
                                   kind="ExternalInput").ap())
    for i, shape in enumerate(_OUTS):
        args.append(nc.dram_tensor(f"out_{i}_dram", shape, _mybir.dt.float32, kind="ExternalOutput").ap())
    hybrid_step(nc, *args)
    r = _run(nc, [arrays], core_ids=[0])
    return tuple(r.results[0][f"out_{i}_dram"] for i in range(len(_OUTS)))
```

```python
from contextlib import ExitStack

import concourse.bass as bass
from concourse import mybir

F32 = mybir.dt.float32
F32R = mybir.dt.float32r
BF16 = mybir.dt.bfloat16
ALU = mybir.AluOpType
ACT = mybir.ActivationFunctionType
AX = mybir.AxisListType

P = 128
D = 1024
KT = D // P
SEQ = 2048
BLK = 512
NBLK = SEQ // BLK
TT = BLK // P
H = 4
HW = H * P
NB = 8
R = NB + 1
NMOD = 6
DFF = 2816
FT = DFF // P
N_IN = 6 * HW + 2 * H
Q0, K0, V0, O0, GATE0 = 0, HW, 2 * HW, 3 * HW, 4 * HW
U0 = GATE0 + 2 * H
S0 = U0 + HW
EPS = 1e-6
QSCALE = float(P) ** -0.5
MASKED = -1.0e30

IN_COLS = [c0 + P * i for c0 in (V0, K0, Q0, S0, O0, U0) for i in range(H)]
N_WIN = len(IN_COLS)
N_OUT = KT
S_OUT = N_WIN
S_UP = S_OUT + N_OUT
S_DOWN = S_UP + 2 * FT
DOWN_K = [(0, 6), (6, 11), (11, 17), (17, 22)]
ND = len(DOWN_K)
NSLAB = S_DOWN + ND * KT

PRE = [0, 1, 2, 3, "R1", 4, "V0", "R2", 5, "V1", "R3", 6, "V2", 7, "R4", "V3", 8, 9, "COL", 10, "WD", 11]
MIX = ["A0", 12, "B0", 13, "A1", 14, "B1", 15, "GV", "A2", 16, "B2", 17, "VST", 18, "A3", 19, "SO", "B3",
       20, "CMS", "CU0", 21, "CU1", "ML", 22, "CU2", 23, "CU3"]

FIRST = {0: ("SG",), 1: ("SW", "SB"), 3: ("SC", "SV"), 4: ("C0", "SH"), 5: ("C1",), 6: ("C2",),
         7: ("C3", "C4"), 8: ("C5", "C6"), 9: ("C7",), 10: ("SQ",), 11: ("ST", "SN"), 12: ("SX",)}

PR_G1, PR_G2, PR_HEAD, PR_LNG, PR_GF = 0, 8, 16, 20, 24
NPR = 32


class Signal:

    def __init__(self, sem, per=0, before=0):
        self.sem, self.per, self.before = sem, per, before

    def at(self, blk, n):
        return blk * self.per + (self.before + n)


def hybrid_step(nc, x_prompt, x_sample, c_prompt, c_sample, state_C, state_n, state_m, w_ada, b_ada,
                g_norm1, w_in, b_gate, g_head, ln_g, ln_b, w_s, b_s, w_out, g_norm2, w_gate_up,
                w_down, g_final, y_prompt, y_sample, C_prompt, n_prompt, m_prompt, C_sample, n_sample,
                m_sample, vs_sample):
    ctx = ExitStack()
    with ctx:
        base = 16512

        def place(name, shape, dt, at):
            return nc.alloc_sbuf_tensor_at(name, shape, dt, offset=base + at)

        top = [0]

        def new(name, shape, dt):
            n = 4 if dt != BF16 else 2
            for s in shape[1:]:
                n *= s
            at = top[0]
            top[0] += (n + 31) // 32 * 32
            return place(name, shape, dt, at), at

        hT_hi, HT = new("hT_hi", [P, KT, BLK], F32R)
        hT_lo, _ = new("hT_lo", [P, KT, BLK], F32R)
        act_hi, U = new("act_hi", [P, FT, BLK], F32R)
        act_lo, _ = new("act_lo", [P, FT, BLK], F32R)
        x_sb, X = new("x_sb", [P, TT, D], F32)
        x1, X1 = new("x1", [P, TT, D], F32)
        work, WK = new("work", [P, 4, BLK], F32)
        raw, _ = new("raw", [P, 2, KT, P], F32)
        w_hi, WH = new("w_hi", [P, 2, KT, P], F32R)
        w_lo, WL = new("w_lo", [P, 2, KT, P], F32R)
        kb = 1024
        qT = place("qT", [P, H, BLK], F32, U)
        kT = place("kT", [P, H, BLK], F32, U + 8 * kb)
        vT = place("vT", [P, H, BLK], F32, U + 16 * kb)
        v_tm = place("v_tm", [P, TT, H, P], F32, U + 24 * kb)
        sigT = place("sigT", [P, H, BLK], F32, U + 32 * kb)
        uT = place("uT", [P, H, BLK], F32, U + 40 * kb)
        vsT = place("vsT", [P, H, BLK], F32, U + 48 * kb)
        mix_hi = place("mix_hi", [P, 2 * H, BLK], F32R, U + 56 * kb)
        mix_lo = place("mix_lo", [P, 2 * H, BLK], F32R, U + 72 * kb)
        rows = place("rows", [P, 8, BLK], F32, U + 32 * kb)
        vs_tm = place("vs_tm", [P, TT, H, P], F32, U + 56 * kb)
        hm = place("hm", [P, TT, H, P], F32, U + 16 * kb)
        E_sb = place("E_sb", [P, H, P], F32, X1)
        P_sb = place("P_sb", [P, H, P], F32, X1 + 2 * kb)
        vg = place("vg", [P, H, P], F32, X1 + 4 * kb)
        k_tm = place("k_tm", [P, H, P], F32, X1 + 6 * kb)
        col = place("col", [P, TT, P], F32, X1 + 8 * kb)
        RT = place("RT", [P, BLK], F32, X1 + 10 * kb)
        R1 = place("R1", [P, BLK], F32, X1 + 12 * kb)
        CT, _ = new("CT", [P, H, P], F32)
        NT, _ = new("NT", [P, H], F32)
        modS, _ = new("modS", [P, 4, KT, NB], F32)
        xsT, _ = new("xsT", [P, KT, NB], F32)
        s_mix, _ = new("s_mix", [P, 2 * H, 2, NB], F32R)
        mst, _ = new("mst", [P, TT + 1], F32)
        sel, _ = new("sel", [P, H, P], F32)
        last_row, _ = new("last_row", [P, P], F32)
        wT, _ = new("wT", [P, H, P], F32)
        bias_cm, _ = new("bias_cm", [P, H, P], F32)
        g_fin, _ = new("g_fin", [P, D], F32)
        mask, _ = new("mask", [P, P], BF16)
        identb, _ = new("identb", [P, P], BF16)
        ident, _ = new("ident", [P, P], F32)
        gw_hi, _ = new("gw_hi", [P, KT * 36 + 92], F32R)
        gw_lo, _ = new("gw_lo", [P, KT * 36 + 92], F32R)
        modT, _ = new("modT", [P, NMOD * KT], F32)
        prmT, _ = new("prmT", [P, NPR], F32)
        A1, _ = new("A1", [P, KT], F32)
        A2, _ = new("A2", [P, KT], F32)
        gb, _ = new("gb", [P, 1], F32)
        onecol, _ = new("onecol", [P, 1], F32)
        onerow, _ = new("onerow", [P, P], F32)
        zrow, _ = new("zrow", [H, P], F32)
        half, _ = new("half", [P, 32], F32)
        dg, DG = new("dg", [P, TT, P], F32)
        junk = place("junk", [P, D], BF16, DG)
        ssum, _ = new("ssum", [P, 2, TT], F32)
        ssall, _ = new("ssall", [P, TT], F32)
        msq, _ = new("msq", [P, TT], F32)
        rrt, _ = new("rrt", [P, TT], F32)
        WD, _ = new("WD", [P, TT, H], F32)
        dd, _ = new("dd", [P, 4, H], F32)
        SS, _ = new("SS", [P, TT, H], F32)
        SSm, _ = new("SSm", [P, TT, H], F32)
        rml, _ = new("rml", [P, TT, H], F32)
        bst, _ = new("bst", [P, H, 6], F32)
        MV, _ = new("MV", [P, TT, H, 2], F32)
        lnv, _ = new("lnv", [P, TT, H], F32)
        rln, _ = new("rln", [P, TT, H], F32)
        assert base + top[0] <= 229344, top[0]

        s_off = [0]

        def beside(name, shape, dt=F32):
            n = 4
            for w in shape:
                n *= w
            s_off[0] += n
            return place(name, [P] + shape, dt, X + s_off[0] - n)

        s_ps = beside("s_ps", [2, FT, 2, NB])
        s_g = beside("s_g", [FT, NB])
        s_u = beside("s_u", [FT, NB])
        s_a = beside("s_a", [FT, NB])
        s_act = beside("s_act", [FT, 2, NB], F32R)
        s_h = beside("s_h", [KT, 2, NB], F32R)
        s_x1, s_x2, s_sq, s_t, s_t2, s_h32 = (beside(n, [KT, NB]) for n in
                                              ("s_x1", "s_x2", "s_sq", "s_t", "s_t2", "s_h32"))
        s_sum, s_ms, s_r = (beside(n, [NB]) for n in ("s_sum", "s_ms", "s_r"))
        s_y = beside("s_y", [D])
        C_end = beside("C_end", [H, P])
        n_end = beside("n_end", [P])
        assert s_off[0] <= TT * D * 4

        stage = place("stage", [P, 4, KT * 512], F32, U)
        proj = place("proj", [NB, N_IN], F32, U + 64 * kb)
        mod = place("mod", [R, NMOD * D], F32, HT)
        hTs = place("hTs", [P, KT, R], F32, HT + 24 * kb)
        h1T = place("h1T", [P, KT, NB], F32, HT + 26 * kb)
        mixTs = place("mixTs", [P, 2 * H, NB], F32, X1 + 15 * kb + 768)
        prm = place("prm", [NPR, P], F32, HT + 27 * kb)
        C0 = place("C0", [P, NB, H, P], F32, U + 48 * kb)
        hrow = place("hrow", [NB, D], F32, X1)
        g1b = place("g1b", [NB, D], F32, WL)
        sel8 = place("sel8", [NB, NB, P], F32, X1 + 4 * kb)
        lnrow = place("lnrow", [NB, 2, HW], F32, U + 77 * kb)
        xs = place("xs", [R, D], F32, WK)
        tmp = place("tmp", [P, D], F32, U + 84 * kb)
        w_raw = place("w_raw", [P, H, P], F32, WH)
        gw_raw = place("gw_raw", [P, KT * 36 + 92], F32, WH + 2 * kb)
        lnb_lh = place("lnb_lh", [2, H, P], F32, WH + 4 * kb)
        cmb_rh = place("cmb_rh", [2, H, P], F32, WH + 6 * kb)
        n0 = place("n0", [NB, H, P], F32, X1 + 8 * kb)
        bcx = place("bcx", [NB, 4, H, NB], F32, X1 + 14 * kb)
        colq = place("colq", [P, 16, H, NB], F32, U + 81 * kb)
        sm = {}
        sm_at = [X1 + 14 * kb + 512]
        for n, w in (("g", 8), ("bg", 8), ("nA", 4), ("e", 4), ("l", 4), ("lf", 4), ("mi", 4), ("m", 4),
                     ("m0", 4), ("em", 4), ("qk", 4), ("nq", 4), ("den", 4), ("den2", 4), ("quant", 16),
                     ("sums", 1), ("mean2", 1), ("r", 1), ("w00", 4), ("bs0", 4), ("mean", 4), ("var", 4),
                     ("rv", 4)):
            sm[n] = place("sm_" + n, [NB, w], F32, sm_at[0])
            sm_at[0] += 32 if w <= 8 else 64
        assert sm_at[0] <= X1 + 15 * kb + 768
        assert base + top[0] <= 229344, top[0]

        bank = [ctx.enter_context(nc.psum_tensor(f"bank{i}", [P, 512], F32)) for i in range(8)]
        G = bank[0:2]
        T = bank[2:4]
        SP_, EP_, N1, N2 = bank[4:8]

        Q_BANK = [N1, EP_, N1, EP_, N1, EP_, N1, N1]
        K_BANK = [N2, SP_, N2, SP_, N2, SP_, N2, N2]
        VST_BANK = [T[0], T[1], N1, N2]
        ML_BANK = [T[0], T[1], SP_, EP_]
        CMS_BANK = [SP_, EP_, N1, N2]
        NT_BANK = [SP_, EP_, N1, N2]

        sems = {}

        def sem(name):
            if name not in sems:
                sems[name] = ctx.enter_context(nc.semaphore(name))
            return sems[name]

        def signal(name, per, before=0):
            return Signal(sem(name), per, before)

        raw_in = [signal(f"raw_in{i}", 16 * NSLAB // 2) for i in range(2)]
        hi_done = signal("hi_done", NSLAB)
        lo_done = signal("lo_done", NSLAB)
        slab_used = signal("slab_used", NSLAB, 1)
        evac = signal("evac", N_WIN + N_OUT + FT + KT, 1)
        silu_done = signal("silu_done", FT, 1)
        gated = signal("gated", FT, 1)
        act_hi_done = signal("act_hi_done", FT)
        act_ready = signal("act_ready", FT)
        ztr = signal("ztr", 2 * KT, 2)
        zadd = signal("zadd", 2 * KT, 2)
        x_in = signal("x_in", 16)
        x_next = signal("x_next", 1)
        squared = signal("squared", 4 * TT, TT)
        ms = signal("ms", 3, 1)
        rs = signal("rs", 3, 1)
        dg_done = signal("dg_done", 2, 1)
        trx = signal("trx", 2 * KT, KT)
        h32 = signal("h32", 2 * KT, KT)
        h_ready = signal("h_ready", 2 * KT, KT + 2)
        y_done = signal("y_done", 1)
        y_out = signal("y_out", 16)
        x1_free = signal("x1_free", 1)
        gates_ps = signal("gates_ps", 1)
        row_n = signal("row_n", 1)
        row_l = signal("row_l", 1)
        row_m = signal("row_m", 1)
        rt_ready = signal("rt_ready", 1)
        col_ps = signal("col_ps", 1)
        col_done = signal("col_done", 1)
        wd_ps = signal("wd_ps", 1)
        wd_done = signal("wd_done", 1)
        vtr = signal("vtr", TT)
        vtm_done = signal("vtm_done", TT)
        ktr = signal("ktr", TT)
        row_e = signal("row_e", 1)
        a_done = signal("a_done", TT)
        ktm_done = signal("ktm_done", TT)
        e_done = signal("e_done", TT)
        p_ready = signal("p_ready", TT)
        vg_done = signal("vg_done", TT)
        b_done = signal("b_done", TT)
        num_done = signal("num_done", TT)
        den_read = signal("den_read", TT)
        ct_done = signal("ct_done", TT, 1)
        ssm_done = signal("ssm_done", 1)
        rml_done = signal("rml_done", 1)
        vstr = signal("vstr", TT)
        vstm_done = signal("vstm_done", TT)
        lnv_done = signal("lnv_done", 1)
        rln_done = signal("rln_done", 1)
        vn_done = signal("vn_done", 1)
        gv_done = signal("gv_done", 1)
        so_done = signal("so_done", 1)
        cms = signal("cms", H)
        hm_done = signal("hm_done", 1)
        hmtr = signal("hmtr", H)
        cms_read = signal("cms_read", H)
        mix_ready = signal("mix_ready", H)
        cu_ready = signal("cu_ready", H)

        block = ctx.enter_context(nc.Block())

        def each_head(ap, n=P):
            return ap.unsqueeze(2).broadcast_to([ap.shape[0], ap.shape[1], n])

        ada_v = w_ada[0].rearrange("(k p) n -> p k n", p=P)
        in_v = w_in[0].rearrange("(k p) n -> p k n", p=P)
        out_v = w_out[0].rearrange("(k p) n -> p k n", p=P)
        up_v = w_gate_up[0].rearrange("(k p) n -> p k n", p=P)
        down_v = w_down[0].rearrange("(k p) n -> p k n", p=P)

        N_ADA = NMOD * D // 512
        thin_in_cols = [(Q0, HW), (K0, HW), (V0, HW), (O0, HW), (U0, HW), (S0, HW), (GATE0, 2 * H)]
        TH_IN = N_ADA
        thin_in = [signal(f"thin_in{i}", 0) for i in range(4)]
        thin_used = signal("thin_used", 0, 4)
        thin_ev = signal("thin_ev", 0, 2)

        def stage_of(t, nk, n):
            return stage[:, t % 4, 0:nk * n].rearrange("p (k n) -> p k n", k=nk)

        @block.sync
        def _(sp):
            sp.dma_start(xs[0:NB, :], c_sample).then_inc(sem("c_in"), 16)
            sp.dma_start(xs[NB:R, :], c_prompt).then_inc(sem("cp_in"), 16)
            sp.dma_start(mod[:, :], b_ada.broadcast_to([R, NMOD * D]))\
                .then_inc(sem("bada_in"), 16)

            def thin_load(t, view, k0, k1, c, n, tt=None):
                sp.wait_ge(thin_used.sem, thin_used.at(0, -3) + (t if tt is None else tt))
                sp.dma_start(stage_of(t, k1 - k0, n), view[:, k0:k1, c]).then_inc(thin_in[t % 4].sem, 16)

            with sp.Fori(0, N_ADA // 4) as i:
                for u in range(4):
                    thin_load(u, ada_v, 0, KT, bass.ds(i * 2048 + u * 512, 512), 512, i * 4 + u)
            for j, (c, n) in enumerate(thin_in_cols):
                thin_load(TH_IN + j, in_v, 0, KT, slice(c, c + n), n)
            def load(blk, s, src, nk):
                if blk is not None:
                    sp.wait_ge(lo_done.sem, lo_done.at(blk, s - 1))
                sp.dma_start(raw[:, s % 2, 0:nk, :], src).then_inc(raw_in[s % 2].sem, 16)

            def load_in(blk, s):
                c = IN_COLS[s % NSLAB]
                load(blk, s, in_v[:, :, c:c + P], KT)

            load_in(None, 0)
            load_in(None, 1)
            with sp.Fori(0, NBLK) as blk:
                for s in range(2, N_WIN):
                    load_in(blk, s)
                with sp.Fori(0, N_OUT // 2) as i:
                    for u in range(2):
                        sp.wait_ge(lo_done.sem, lo_done.at(blk, S_OUT + u - 1) + i * 2)
                        sp.dma_start(raw[:, u, :, :], out_v[:, :, bass.ds(i * (2 * P) + u * P, P)])\
                            .then_inc(raw_in[u].sem, 16)
                with sp.Fori(0, FT) as i:
                    for u in range(2):
                        sp.wait_ge(lo_done.sem, lo_done.at(blk, S_UP + u - 1) + i * 2)
                        sp.dma_start(raw[:, u, :, :], up_v[:, :, bass.ds(i * P + u * DFF, P)])\
                            .then_inc(raw_in[u].sem, 16)
                with sp.Fori(0, KT) as i:
                    for q, (k0, k1) in enumerate(DOWN_K):
                        sp.wait_ge(lo_done.sem, lo_done.at(blk, S_DOWN + q - 1) + i * ND)
                        sp.dma_start(raw[:, q % 2, 0:k1 - k0, :], down_v[:, k0:k1, bass.ds(i * P, P)])\
                            .then_inc(raw_in[q % 2].sem, 16)
                for s in (NSLAB, NSLAB + 1):
                    load_in(blk, s)
            y_last = y_prompt[0].rearrange("(b i p) d -> b p i d", p=P, i=TT)[NBLK - 1]
            for i in range(TT):
                sp.wait_ge(sem("y_row"), i + 1)
                sp.dma_start(y_last[:, i, :], x1[:, i, :]).then_inc(sem("y_rows_out"), 16)
            sp.wait_ge(sem("y_rows_out"), 16 * TT)
            for i in range(2):
                sp.wait_ge(raw_in[i].sem, raw_in[i].at(NBLK, 16))

        @block.gpsimd
        def _(pool):
            pool.memset(half[:, :], -0.5).then_inc(sem("half_set"), 1)
            pool.memset(ident[:, :], 0.0).then_inc(sem("z_ident"), 1)
            pool.memset(identb[:, :], 0.0).then_inc(sem("z_ident"), 1)
            pool.memset(mask[:, :], 0.0).then_inc(sem("z_ident"), 1)
            pool.memset(last_row[:, :], 0.0).then_inc(sem("z_ident"), 1)
            pool.memset(sel[:, :, :], 0.0).then_inc(sem("z_ident"), 1)
            pool.wait_ge(sem("z_ident"), 5)
            for m in (ident, identb):
                pool.affine_select(out=m[:, :], in_=m[:, :], compare_op=ALU.not_equal, fill=1.0, base=0,
                                   pattern=[[-1, P]], channel_multiplier=1).then_inc(sem("consts"), 1)
            pool.affine_select(out=mask[:, :], in_=mask[:, :], compare_op=ALU.is_ge, fill=MASKED, base=0,
                               pattern=[[1, P]], channel_multiplier=-1).then_inc(sem("consts"), 1)
            pool.affine_select(out=last_row[:, :], in_=last_row[:, :], compare_op=ALU.not_equal, fill=1.0,
                               base=-(P - 1), pattern=[[0, P]], channel_multiplier=1)\
                .then_inc(sem("consts"), 1)
            pool.affine_select(out=sel[:, :, :], in_=sel[:, :, :], compare_op=ALU.not_equal, fill=1.0,
                               base=0, pattern=[[-1, H], [0, P]], channel_multiplier=1)\
                .then_inc(sem("consts"), 1)
            pool.wait_ge(sem("ws_in"), 16)
            pool.affine_select(out=w_raw[:, :, :], in_=w_raw[:, :, :], compare_op=ALU.is_ge, fill=0.0,
                               base=0, pattern=[[0, H], [-1, P]], channel_multiplier=1)\
                .then_inc(sem("ws_masked"), 1)

            def power(done, out, src, width, rows):
                pool.tensor_tensor(out, src, half[0:rows, 0:width], ALU.pow).then_inc(done, 1)

            x_v = x_prompt[0].rearrange("(b i p) d -> b p i d", p=P, i=TT)
            y_v = y_prompt[0].rearrange("(b i p) d -> b p i d", p=P, i=TT)
            pool.wait_ge(thin_used.sem, thin_used.at(0, N_ADA // 2))
            pool.dma_start(x_sb[:, :, :], x_v[0]).then_inc(x_in.sem, 16)

            def root(blk, n):
                pool.wait_ge(ms.sem, ms.at(blk, n + 1))
                power(rs.sem, rrt[:, :], msq[:, :], TT, P)

            pool.wait_ge(sem("half_set"), 1)
            pool.wait_ge(sem("ms1s"), 1)
            power(sem("r1s"), sm["r"][:, :], sm["mean2"][:, :], 1, NB)
            root(0, -1)
            def pool_block(blk, last):
                for c in range(TT):
                    if c == 0:
                        pool.wait_ge(col_done.sem, col_done.at(blk, 1))
                    else:
                        pool.wait_ge(b_done.sem, b_done.at(blk, c))
                    pool.wait_ge(vtm_done.sem, vtm_done.at(blk, c + 1))
                    wg = each_head(col[:, c, 96:96 + H])
                    pool.tensor_tensor(vg[:, :, :], v_tm[:, c], wg, ALU.mult).then_inc(vg_done.sem, 1)
                by_row = lambda a: a[:, :, :].rearrange("p c h -> p (c h)")
                for src_done, src, root_done, roots, x, done in (
                        (lnv_done, lnv, rln_done, rln, vs_tm, vn_done),
                        (ssm_done, SSm, rml_done, rml, hm, hm_done)):
                    pool.wait_ge(src_done.sem, src_done.at(blk, 1))
                    power(root_done.sem, by_row(roots), by_row(src), TT * H, P)
                    pool.wait_ge(root_done.sem, root_done.at(blk, 1))
                    v = x[:, :, :, :].rearrange("p c h e -> p (c h) e")
                    pool.tensor_tensor(v, v, each_head(by_row(roots)), ALU.mult).then_inc(done.sem, 1)
                root(blk, 0)
                if last:
                    sample_root(1)
                    state_out()
                if not last:
                    pool.wait_ge(zadd.sem, zadd.at(blk, KT))
                    pool.dma_start(x_sb[:, :, :], x_v[bass.ds(blk + 1, 1)].rearrange("o p i d -> p (o i) d"))\
                        .then_inc(x_in.sem, 16)
                    pool.wait_ge(x_in.sem, x_in.at(blk, 32))
                    pool.sem_inc(x_next.sem, 1)
                    root(blk, 1)
                root(blk, 1 if last else 2)
                if last:
                    sample_root(2)
                else:
                    pool.wait_ge(y_done.sem, y_done.at(blk, 1))
                    pool.dma_start(y_v[bass.ds(blk, 1)].rearrange("o p i d -> p (o i) d"), x1[:, :, :])\
                        .then_inc(y_out.sem, 16)
                    pool.wait_ge(y_out.sem, y_out.at(blk, 16))
                    pool.sem_inc(x1_free.sem, 1)

            def state_out():
                pool.dma_start(m_prompt[0].rearrange("o h -> h o"), mst[0:H, 0:1])\
                    .then_inc(sem("fin_out"), 16)
                pool.wait_ge(sem("fin_set"), 1)
                pool.dma_start(C_prompt[0, 0].rearrange("h e d -> e h d"), C_end[:, :, :])\
                    .then_inc(sem("fin_out"), 16)
                pool.dma_start(n_prompt[0, 0], n_end[0:H, :]).then_inc(sem("fin_out"), 16)

            def sample_root(n):
                pool.wait_ge(sem("s_mean"), n)
                power(sem("s_root"), s_r[:, :], s_ms[:, :], NB, P)

            pool.sem_inc(x1_free.sem, 1)
            pool.wait_ge(sem("vars"), 1)
            power(sem("rvs"), sm["rv"][:, :], sm["var"][:, :], H, NB)
            pool.wait_ge(sem("msml"), 1)
            power(sem("rmls"), colq[:, 9].rearrange("p h b -> p (h b)"),
                  colq[:, 8].rearrange("p h b -> p (h b)"), H * NB, P)
            with pool.Fori(0, NBLK - 1) as blk:
                pool_block(blk, False)
            pool_block(NBLK - 1, True)
            pool.wait_ge(sem("fin_out"), 48)

        @block.scalar
        def _(act):
            def fetch(name, dst, src, single=False):
                act.dma_start(dst, src, allow_slow_non_contiguous=single).then_inc(sem(name), 16)

            act.wait_ge(sem("c_in"), 16)
            act.wait_ge(sem("cp_in"), 16)
            act.activation(xs[:, :], xs[:, :], ACT.Silu).then_inc(sem("c_silu"), 1)
            fetch("prm_in", prm[PR_G1:PR_G1 + KT, :], g_norm1[0].rearrange("(k p) -> k p", p=P))
            fetch("prm_in", prm[PR_G2:PR_G2 + KT, :], g_norm2[0].rearrange("(k p) -> k p", p=P))
            fetch("prm_in", prm[PR_HEAD:PR_HEAD + H, :], g_head[0])
            fetch("prm_in", prm[PR_LNG:PR_LNG + H, :], ln_g[0])
            fetch("prm_in", prm[PR_GF:PR_GF + KT, :], g_final.rearrange("(k p) -> k p", p=P))
            fetch("ws_in", w_raw[:, :, :], w_s[0].rearrange("h t s -> t h s"))
            act.wait_ge(sem("lh_one"), 1)
            fetch("cmb_in", lnb_lh[0:1, :, :], ln_b)
            fetch("cmb_in", cmb_rh[1:2, :, :], b_s)
            act.wait_ge(sem("gw_zero"), 1)
            gcols = gw_raw[:, 0:KT * 36].rearrange("p (k c) -> p k c", c=36)
            fetch("gw_in", gcols[:, :, 0:H], in_v[:, :, GATE0:GATE0 + H])
            fetch("gw_in", gcols[:, :, 32:32 + H], in_v[:, :, GATE0 + H:GATE0 + 2 * H])
            act.wait_ge(sem("gb_zero"), 1)
            fetch("gb_in", gb[0:H, :], b_gate[0, 0:H].rearrange("(h o) -> h o", o=1))
            fetch("gb_in", gb[32:32 + H, :], b_gate[0, H:2 * H].rearrange("(h o) -> h o", o=1))
            fetch("srow_in", g1b[:, :], g_norm1.broadcast_to([NB, D]))
            fetch("srow_in", lnrow[:, 0, :], ln_g.rearrange("o h e -> o (h e)").broadcast_to([NB, HW]))
            fetch("srow_in", lnrow[:, 1, :], ln_b.rearrange("o h e -> o (h e)").broadcast_to([NB, HW]))
            fetch("srow_in", sm["bg"][:, :], b_gate.broadcast_to([NB, 2 * H]))
            fetch("srow_in", sm["m0"][:, :], state_m[0])
            fetch("srow_in", n0[:, :, :], state_n[0])
            fetch("srow_in", sm["w00"][:, :], w_s[:, :, 0, 0].broadcast_to([NB, H]), True)
            fetch("srow_in", sm["bs0"][:, :], b_s[:, :, 0].broadcast_to([NB, H]), True)
            fetch("gf_in", g_fin[:, :], g_final.rearrange("(o d) -> o d", o=1).broadcast_to([P, D]))

            def squares(blk, n, x_tiles, c0=0, c1=D, part=0, rows=range(TT)):
                if n >= 0:
                    act.wait_ge(ms.sem, ms.at(blk, n))
                before = {-1: -TT, 0: 0, 1: 2 * TT, 2: 3 * TT}[n] + part * TT
                for i in rows:
                    if n >= 0 or i > 0:
                        act.wait_ge(squared.sem, squared.at(blk, before + i))
                    act.activation(junk[:, c0:c1], x_tiles[:, i, c0:c1], ACT.Square,
                                   accum_out=ssum[:, part, i:i + 1]).then_inc(squared.sem, 1)

            act.wait_ge(sem("cT_ps"), 1)
            fetch("xs_in", xs[0:NB, :], x_sample.rearrange("b s d -> (b s) d"))

            def sample_squares(done):
                act.activation(tmp[0:NB, :], xs[0:NB, :], ACT.Square, accum_out=sm["sums"][:, :])\
                    .then_inc(done, 1)

            act.wait_ge(sem("xs_in"), 16)
            sample_squares(sem("ss1s"))
            act.wait_ge(x_in.sem, 16)
            squares(0, -1, x_sb)
            act.wait_ge(thin_used.sem, thin_used.at(0, N_ADA + 4))
            fetch("C_in", C0[:, :, :, :], state_C[0].rearrange("b h e d -> e b h d"))
            def for_samples(step):
                if step == "SG":
                    act.wait_ge(sem("nAs"), 1)
                    act.activation(sm["e"][:, :], sm["nA"][:, :], ACT.Exp).then_inc(sem("es"), 1)
                    act.wait_ge(sem("es"), 1)
                    act.activation(sm["l"][:, :], sm["e"][:, :], ACT.Ln, bias=1.0).then_inc(sem("ls"), 1)
                elif step == "SW":
                    act.wait_ge(sem("wargs"), 1)
                    act.activation(sm["quant"][:, 4:12], sm["quant"][:, 4:12], ACT.Exp)\
                        .then_inc(sem("wexp"), 1)
                    act.activation(sm["em"][:, :], sm["m"][:, :], ACT.Exp, scale=-1.0)\
                        .then_inc(sem("wexp"), 1)
                    fetch("small_out", m_sample[0], sm["m"][:, :])
                elif step == "SB":
                    act.activation(proj[:, U0:U0 + 2 * HW], proj[:, U0:U0 + 2 * HW], ACT.Gelu_apprx_tanh)\
                        .then_inc(sem("gelus"), 1)
                elif step == "SC":
                    act.wait_ge(sem("oTs"), 1)
                    act.activation(colq[:, 10], colq[:, 1], ACT.Sigmoid).then_inc(sem("sigs"), 1)
                    act.wait_ge(sem("n_new"), 1)
                    fetch("small_out", n_sample[0], n0[:, :, :])
                elif step == "SN":
                    act.wait_ge(sem("vs_new"), 1)
                    fetch("thin_out", vs_sample[0].rearrange("b s h e -> (b s) (h e)"), proj[:, S0:S0 + HW])
                    act.wait_ge(sem("C_upd"), NB)
                    fetch("thin_out", C_sample[0].rearrange("b h e d -> e b h d"), C0[:, :, :, :])
                elif step[0] == "C":
                    b = int(step[1])
                    act.wait_ge(sem("wv_set"), 1)
                    act.wait_ge(sem("qkb"), b + 1)
                    if b > 0:
                        act.wait_ge(sem("C_upd"), b)
                    for h in range(H):
                        ins = act.activation(tmp[:, HW + h * P:HW + (h + 1) * P], K_BANK[b][:, h * P:(h + 1) * P],
                                             ACT.Copy, scale=colq[:, 3, h, b:b + 1])
                    ins.then_inc(sem("vk_set"), 1)

            def split_hi(blk, s, used=True, j=0):
                act.wait_ge(raw_in[s % 2].sem, raw_in[s % 2].at(blk, 16 * (s // 2 + 1)) + j * 8)
                if used:
                    act.wait_ge(slab_used.sem, slab_used.at(blk, s - 1) + j)
                act.activation(w_hi[:, s % 2], raw[:, s % 2], ACT.Copy).then_inc(hi_done.sem, 1)

            def norm_tile(blk, n, k, a_col, b_col):
                act.wait_ge(trx.sem, trx.at(blk, n * KT + k + 1))
                act.wait_ge(h_ready.sem, h_ready.at(blk, n * KT + k - 1))
                act.activation(work[:, 2 + k % 2], NT_BANK[k % 4][:, :], ACT.Identity,
                               scale=a_col[:, k:k + 1], bias=b_col[:, k:k + 1]).then_inc(h32.sem, 1)

            def mix_slab(blk, s):
                h = s % H
                dst, f, scale = [(vT, ACT.Copy, 1.0), (kT, ACT.Copy, 1.0), (qT, ACT.Copy, QSCALE),
                                 (vsT, ACT.Copy, 1.0), (sigT, ACT.Copy, 1.0),
                                 (uT, ACT.Gelu_apprx_tanh, 1.0)][s // H]
                act.wait_ge(slab_used.sem, slab_used.at(blk, s + 1))
                act.activation(dst[:, h, :], G[s % 2][:, :], f, scale=scale).then_inc(evac.sem, 1)

            def gate_log(blk):
                act.wait_ge(row_n.sem, row_n.at(blk, 1))
                act.activation(rows[0:H, 3, :], rows[0:H, 2, :], ACT.Exp).then_inc(row_e.sem, 1)
                act.wait_ge(row_e.sem, row_e.at(blk, 1))
                act.activation(rows[0:H, 4, :], rows[0:H, 3, :], ACT.Ln, bias=1.0).then_inc(row_l.sem, 1)

            def gate_weights(blk):
                act.wait_ge(row_m.sem, row_m.at(blk, 1))
                for c in range(TT):
                    t = slice(c * P, (c + 1) * P)
                    act.activation(RT[32:32 + H, t], rows[0:H, 6, t], ACT.Exp, scale=-1.0,
                                   bias=mst[0:H, c:c + 1])
                    act.activation(RT[96:96 + H, t], RT[0:H, t], ACT.Exp,
                                   bias=R1[0:H, (c + 1) * P - 1:(c + 1) * P])
                act.activation(RT[64:64 + H, :], rows[0:H, 7, :], ACT.Exp, scale=-1.0)\
                    .then_inc(rt_ready.sem, 1)

            def chunk_a(blk, c):
                act.wait_ge(ktr.sem, ktr.at(blk, c + 1))
                if c > 0:
                    act.wait_ge(b_done.sem, b_done.at(blk, c))
                act.activation(k_tm[:, :, :], T[0][:, :], ACT.Copy).then_inc(ktm_done.sem, 1)
                act.wait_ge(a_done.sem, a_done.at(blk, c + 1))
                if c > 0:
                    act.wait_ge(p_ready.sem, p_ready.at(blk, c))
                for h in range(H):
                    ins = act.activation(E_sb[:, h, :], EP_[:, h * P:(h + 1) * P], ACT.Exp,
                                         bias=col[:, c, h:h + 1])
                ins.then_inc(e_done.sem, 1)

            def act_block(blk, last, first=False):
                for step in PRE + MIX:
                    if isinstance(step, int):
                        if first and step == N_WIN // 2:
                            act.wait_ge(sem("thin_out"), 32)
                        mix_slab(blk, step)
                        if step + 2 <= N_WIN:
                            split_hi(blk, step + 2)
                        for piece in FIRST.get(step, ()) if first else ():
                            for_samples(piece)
                    elif step == "GV":
                        act.wait_ge(evac.sem, evac.at(blk, 4 * H))
                        act.activation(vsT[:, :, :], vsT[:, :, :], ACT.Gelu_apprx_tanh)\
                            .then_inc(gv_done.sem, 1)
                    elif step == "SO":
                        act.wait_ge(evac.sem, evac.at(blk, 5 * H))
                        act.activation(sigT[:, :, :], sigT[:, :, :], ACT.Sigmoid).then_inc(so_done.sem, 1)
                    elif step == "R2":
                        gate_log(blk)
                    elif step == "R4":
                        gate_weights(blk)
                    elif step[:-1] == "V":
                        c = int(step[1])
                        act.wait_ge(vtr.sem, vtr.at(blk, c + 1))
                        act.activation(v_tm[:, c], T[c % 2][:, :], ACT.Copy).then_inc(vtm_done.sem, 1)
                    elif step[:-1] == "A":
                        chunk_a(blk, int(step[1]))
                with act.Fori(0, N_OUT // 2 - 1) as i:
                    for u in range(2):
                        split_hi(blk, S_OUT + u + 1, j=i * 2)
                        out_gate(blk, i, u, S_OUT + u + 1, 2, 0, modT, 2 * KT)
                split_hi(blk, S_OUT + 7)
                out_gate(blk, 3, 0, S_OUT + 1, 2, 0, modT, 2 * KT)
                split_hi(blk, S_OUT + 8)
                act.wait_ge(zadd.sem, zadd.at(blk, KT - 2))
                squares(blk, 0, x1, 0, D - 2 * P, 0)
                out_gate(blk, 3, 1, S_OUT + 2, 2, 0, modT, 2 * KT)
                act.wait_ge(zadd.sem, zadd.at(blk, KT))
                squares(blk, 0, x1, D - 2 * P, D, 1)
                for k in range(KT):
                    norm_tile(blk, 0, k, A2, modT[:, 3 * KT:4 * KT])
                split_hi(blk, S_UP + 1)
                with act.Fori(0, FT) as i:
                    act.wait_ge(slab_used.sem, slab_used.at(blk, S_UP + 1) + i * 2)
                    act.wait_ge(gated.sem, gated.at(blk, 0) + i)
                    act.activation(work[:, 2], G[0][:, :], ACT.Sigmoid).then_inc(evac.sem, 1)
                    split_hi(blk, S_UP + 2, j=i * 2)
                    act.wait_ge(gated.sem, gated.at(blk, 1) + i)
                    act.activation(act_hi[:, bass.ds(i, 1), :], work[:, 3:4, :], ACT.Copy)\
                        .then_inc(act_hi_done.sem, 1)
                    split_hi(blk, S_UP + 3, j=i * 2)
                if last:
                    act.wait_ge(sem("s_up"), 1)
                    act.activation(s_g[:, :, :], s_g[:, :, :], ACT.Silu).then_inc(sem("s_silu"), 1)

                def split_four(n, j=0):
                    for q in range(ND):
                        split_hi(blk, S_DOWN + ND * n + q + 1, j=j)

                def next_tiles(ks):
                    for k in ks if not last else ():
                        norm_tile(blk, 1, k, A1, modT[:, 0:KT])

                for q in range(ND):
                    if q > 0:
                        split_hi(blk, S_DOWN + q + 1)
                    if q < 2 and not last:
                        act.wait_ge(x_next.sem, x_next.at(blk, 1))
                        squares(blk, 1, x_sb, rows=(2 * q, 2 * q + 1))
                out_gate(blk, 0, 0, S_DOWN + ND, 2 * ND, KT, modT, 5 * KT)
                next_tiles(range(4))
                with act.Fori(0, 3) as i:
                    split_four(1, i * (2 * ND))
                    out_gate(blk, i, 1, S_DOWN + 2 * ND, 2 * ND, KT, modT, 5 * KT)
                    split_four(2, i * (2 * ND))
                    out_gate(blk, i, 2, S_DOWN + 3 * ND, 2 * ND, KT, modT, 5 * KT)
                split_four(7)
                if last:
                    act.wait_ge(zadd.sem, zadd.at(blk, 2 * KT - 2))
                    squares(blk, 1, x1, 0, D - 2 * P)
                out_gate(blk, 3, 1, S_DOWN + 2 * ND, 2 * ND, KT, modT, 5 * KT)
                next_tiles(range(4, 8))
                if not last:
                    split_hi(blk, NSLAB + 1)
                act.wait_ge(zadd.sem, zadd.at(blk, 2 * KT))
                if last:
                    squares(blk, 1, x1, D - 2 * P, D, 1)
                else:
                    squares(blk, 2, x1)

            def out_gate(blk, i, u, done, step, first, gates, g0):
                act.wait_ge(slab_used.sem, slab_used.at(blk, done) + i * step)
                act.wait_ge(ztr.sem, ztr.at(blk, first + u - 1) + i * 2)
                act.activation(work[:, u % 2], G[u % 2][:, :], ACT.Copy,
                               scale=gates[:, bass.ds(i * 2 + (g0 + u), 1)]).then_inc(evac.sem, 1)

            split_hi(0, 0, used=False)
            for k in range(KT):
                norm_tile(0, -1, k, A1, modT[:, 0:KT])
            split_hi(0, 1, used=False)
            act_block(0, False, first=True)
            with act.Fori(1, NBLK - 1) as blk:
                act_block(blk, False)
            act_block(NBLK - 1, True)
            act.wait_ge(sem("s_y_ps"), 1)
            act.activation(s_y[0:NB, 0:BLK], NT_BANK[0][0:NB, :], ACT.Copy).then_inc(sem("s_done"), 1)
            act.wait_ge(sem("s_done"), 2)
            fetch("ys_out", y_sample.rearrange("b s d -> (b s) d"), s_y[0:NB, :])
            act.wait_ge(sem("ys_out"), 16)

        @block.vector
        def _(ve):
            TH_CHAIN, BLK_CHAIN = 200, 400
            chain = signal("ve_chain", BLK_CHAIN, TH_CHAIN)
            at = {"blk": None, "n": 0}

            def link(ins):
                at["n"] += 1
                ins.then_inc(chain.sem, 1)
                if at["blk"] is None:
                    ve.wait_ge(chain.sem, at["n"])
                else:
                    ve.wait_ge(chain.sem, chain.at(at["blk"], at["n"]))

            def round_off(n):
                while at["n"] < n:
                    k = min(n - at["n"], 100)
                    ve.sem_inc(chain.sem, k)
                    at["n"] += k
                assert at["n"] == n, at["n"]

            ve.memset(lnb_lh[:, :, :], 1.0).then_inc(sem("lh_one"), 1)
            ve.memset(gw_raw[:, :], 0.0).then_inc(sem("gw_zero"), 1)
            ve.memset(gb[:, :], 0.0).then_inc(sem("gb_zero"), 1)
            ve.memset(onecol[:, :], 1.0)
            ve.memset(onerow[:, :], 1.0).then_inc(sem("ones"), 1)
            ve.memset(zrow[:, :], 0.0)
            ve.memset(CT[:, :, :], 0.0)
            ve.memset(NT[:, :], 0.0)
            link(ve.memset(mst[:, :], 0.0))
            ve.wait_ge(sem("consts"), 5)
            ve.tensor_copy(sel8[:, :, :], each_head(ident[0:NB, 0:NB])).then_inc(sem("sel8_set"), 1)
            ve.wait_ge(sem("cT_ps"), 1)
            ve.tensor_copy(hTs[:, :, :], T[0][:, 0:KT * R]).then_inc(sem("cT_set"), 1)

            def mean_square(blk, n, parts=1):
                ve.wait_ge(squared.sem, squared.at(blk, {-1: 0, 0: TT, 1: 3 * TT, 2: 4 * TT}[n]
                                                   + (parts - 1) * TT))
                sums = ssum[:, 0, :]
                if parts == 2:
                    link(ve.tensor_tensor(ssall[:, :], ssum[:, 0, :], ssum[:, 1, :], ALU.add))
                    sums = ssall[:, :]
                ve.tensor_scalar(msq[:, :], sums, 1.0 / D, EPS, ALU.mult, ALU.add).then_inc(ms.sem, 1)
                ve.wait_ge(rs.sem, rs.at(blk, n + 1))

            def diagonals(blk, n):
                mean_square(blk, n, 2 if n == 0 else 1)
                ve.tensor_tensor(dg[:, :, :], ident[:, :].unsqueeze(1).broadcast_to([P, TT, P]),
                                 each_head(rrt[:, :]), ALU.mult).then_inc(dg_done.sem, 1)

            ve.wait_ge(sem("bada_in"), 16)
            def sample_norm(sums, mean, root, gain):
                ve.wait_ge(sem(sums), 1)
                ve.tensor_scalar(sm["mean2"][:, :], sm["sums"][:, :], 1.0 / D, EPS, ALU.mult, ALU.add)\
                    .then_inc(sem(mean), 1)
                ve.wait_ge(sem(root), 1)
                ve.wait_ge(sem("srow_in"), 128)
                return ve.scalar_tensor_tensor(out=hrow[:, :], in0=xs[0:NB, :], scalar=sm["r"][:, :],
                                               in1=gain, op0=ALU.mult, op1=ALU.mult)

            def modulate(shift, scale, done):
                link(ve.scalar_tensor_tensor(out=tmp[0:NB, :], in0=mod[0:NB, scale * D:(scale + 1) * D],
                                             scalar=1.0, in1=hrow[:, :], op0=ALU.add, op1=ALU.mult))
                ve.tensor_tensor(hrow[:, :], tmp[0:NB, :], mod[0:NB, shift * D:(shift + 1) * D], ALU.add)\
                    .then_inc(sem(done), 1)

            def sample_columns(ps_ready, done):
                ve.wait_ge(sem(ps_ready), 1)
                ve.tensor_copy(xsT[:, :, :], T[1][:, KT * NB:2 * KT * NB].rearrange("p (k b) -> p k b", b=NB))
                ve.tensor_copy(h1T[:, :, :], T[1][:, 0:KT * NB].rearrange("p (k b) -> p k b", b=NB))\
                    .then_inc(sem(done), 1)

            with ve.Fori(0, N_ADA // 2 - 2) as i:
                for u in range(2):
                    ve.wait_ge(thin_used.sem, thin_used.at(0, u + 1) + i * 2)
                    m = mod[:, bass.ds(i * 1024 + u * 512, 512)]
                    ve.tensor_tensor(m, G[u][0:R, :], m, ALU.add).then_inc(thin_ev.sem, 1)

            def modulation_columns():
                ve.wait_ge(sem("modT_ps"), 1)
                mod_ps = SP_[:, 0:NMOD * KT * R].rearrange("p (m k r) -> p m k r", r=R, k=KT)
                for i, m in ((0, 2), (2, 3), (3, 5)):
                    ve.tensor_copy(modS[:, i], mod_ps[:, m, :, 0:NB])
                ve.scalar_tensor_tensor(out=modS[:, 1], in0=mod_ps[:, 4, :, 0:NB], scalar=1.0,
                                        in1=each_head(prmT[:, PR_G2:PR_G2 + KT], NB), op0=ALU.add, op1=ALU.mult)
                link(ve.tensor_copy(modT[:, :],
                                    SP_[:, 0:NMOD * KT * R].rearrange("p (j r) -> p j r", r=R)[:, :, NB]))
                ve.scalar_tensor_tensor(out=A1[:, :], in0=modT[:, KT:2 * KT], scalar=1.0,
                                        in1=prmT[:, PR_G1:PR_G1 + KT], op0=ALU.add, op1=ALU.mult)
                ve.scalar_tensor_tensor(out=A2[:, :], in0=modT[:, 4 * KT:5 * KT], scalar=1.0,
                                        in1=prmT[:, PR_G2:PR_G2 + KT], op0=ALU.add, op1=ALU.mult)

            def modulation(t):
                ve.wait_ge(thin_used.sem, thin_used.at(0, t + 1))
                m = mod[:, t * 512:(t + 1) * 512]
                ve.tensor_tensor(m, G[t % 2][0:R, :], m, ALU.add).then_inc(thin_ev.sem, 1)

            modulation(N_ADA - 4)
            link(sample_norm("ss1s", "ms1s", "r1s", g1b[:, :]))
            modulate(0, 1, "h1s")
            modulation(N_ADA - 3)
            sample_columns("h1T_ps", "h1T_set")
            ve.wait_ge(sem("prm_ps"), 1)
            link(ve.tensor_copy(prmT[:, :], T[0][:, 0:NPR]))
            ve.wait_ge(sem("gb_in"), 32)
            ve.wait_ge(sem("gw_in"), 32)
            link(ve.tensor_copy(gw_hi[:, :], gw_raw[:, :]))
            ve.tensor_tensor(gw_lo[:, :], gw_raw[:, :], gw_hi[:, :].bitcast(F32), ALU.subtract)
            ve.wait_ge(sem("wT_ps"), 1)
            ve.tensor_copy(wT[:, :, :], N1[:, :]).then_inc(sem("wT_set"), 1)
            modulation(N_ADA - 2)
            ve.wait_ge(sem("rsum_ps"), 1)
            ve.tensor_copy(cmb_rh[0:1, :, :], N2[0:1, :]).then_inc(sem("rsum_set"), 1)
            modulation(N_ADA - 1)
            ve.wait_ge(sem("bcm_ps"), 1)
            ve.tensor_copy(bias_cm[:, :, :], EP_[:, :]).then_inc(sem("bcm_set"), 1)
            diagonals(0, -1)
            for j, (c, n) in enumerate(thin_in_cols):
                ve.wait_ge(thin_used.sem, thin_used.at(0, TH_IN + j + 1))
                link(ve.tensor_copy(proj[:, c:c + n], G[(TH_IN + j) % 2][0:NB, 0:n]))
                ve.sem_inc(thin_ev.sem, 1)
                if j == 1:
                    modulation_columns()
            q8, k8, v8 = (proj[:, c:c + HW] for c in (Q0, K0, V0))
            by_head = lambda a: a.rearrange("b (h e) -> b h e", h=H)
            wi8, wg8, s8, rd8 = (sm["quant"][:, 4 * i:4 * i + 4] for i in (1, 2, 0, 3))
            g = sm["g"]
            ve.sem_inc(sem("proj_set"), 1)
            sT, wiT, wgT, rdT = (colq[:, 12 + i] for i in range(4))
            vs8, u8 = proj[:, S0:S0 + HW], proj[:, U0:U0 + HW]
            ta, tb = hrow[:, 0:HW], hrow[:, HW:2 * HW]

            def for_samples(step):
                if step == "SG":
                    link(ve.tensor_tensor(g[:, :], proj[:, GATE0:GATE0 + 2 * H], sm["bg"][:, :], ALU.add))
                    ve.scalar_tensor_tensor(out=sm["nA"][:, :], in0=g[:, H:2 * H], scalar=-1.0, in1=g[:, H:2 * H],
                                            op0=ALU.mult, op1=ALU.min).then_inc(sem("nAs"), 1)
                elif step == "SW":
                    ve.wait_ge(sem("ls"), 1)
                    link(ve.scalar_tensor_tensor(out=sm["lf"][:, :], in0=g[:, H:2 * H], scalar=0.0,
                                                 in1=sm["l"][:, :], op0=ALU.min, op1=ALU.subtract))
                    link(ve.tensor_tensor(sm["mi"][:, :], sm["lf"][:, :], sm["m0"][:, :], ALU.add))
                    link(ve.tensor_tensor(sm["m"][:, :], sm["mi"][:, :], g[:, 0:H], ALU.max))
                    ve.tensor_tensor(wi8, sm["mi"][:, :], sm["m"][:, :], ALU.subtract)
                    ve.tensor_tensor(wg8, g[:, 0:H], sm["m"][:, :], ALU.subtract).then_inc(sem("wargs"), 1)
                    link(ve.tensor_tensor(tmp[0:NB, 0:HW], q8, k8, ALU.mult))
                    ve.tensor_reduce(sm["qk"][:, :], by_head(tmp[0:NB, 0:HW]), AX.X, ALU.add)
                    link(ve.tensor_tensor(tmp[0:NB, HW:2 * HW], n0[:, :, :].rearrange("b h e -> b (h e)"), q8,
                                          ALU.mult))
                    link(ve.tensor_reduce(sm["nq"][:, :], by_head(tmp[0:NB, HW:2 * HW]), AX.X, ALU.add))
                    ve.wait_ge(sem("wexp"), 2)
                    ve.scalar_tensor_tensor(out=s8, in0=sm["qk"][:, :], scalar=QSCALE, in1=wg8, op0=ALU.mult,
                                            op1=ALU.mult)
                    link(ve.scalar_tensor_tensor(out=sm["den"][:, :], in0=sm["nq"][:, :], scalar=QSCALE, in1=wi8,
                                                 op0=ALU.mult, op1=ALU.mult))
                    link(ve.tensor_tensor(sm["den2"][:, :], sm["den"][:, :], s8, ALU.add))
                    link(ve.scalar_tensor_tensor(out=sm["den"][:, :], in0=sm["den2"][:, :], scalar=-1.0,
                                                 in1=sm["den2"][:, :], op0=ALU.mult, op1=ALU.max))
                    link(ve.tensor_tensor(sm["den2"][:, :], sm["den"][:, :], sm["em"][:, :], ALU.max))
                    link(ve.reciprocal(rd8, sm["den2"][:, :]))
                    ve.tensor_tensor(n0[:, :, :], n0[:, :, :], each_head(wi8), ALU.mult)
                    link(ve.tensor_tensor(by_head(tmp[0:NB, 0:HW]), by_head(k8), each_head(wg8), ALU.mult))
                    ve.tensor_tensor(n0[:, :, :], n0[:, :, :], by_head(tmp[0:NB, 0:HW]), ALU.add)\
                        .then_inc(sem("n_new"), 1)
                elif step == "SB":
                    for i in range(4):
                        ins = ve.tensor_tensor(bcx[:, i, :, :],
                                               ident[0:NB, 0:NB].unsqueeze(1).broadcast_to([NB, H, NB]),
                                               sm["quant"][:, 4 * i:4 * i + 4].unsqueeze(2)
                                               .broadcast_to([NB, H, NB]), ALU.mult)
                    ins.then_inc(sem("bcx_set"), 1)
                elif step == "SC":
                    ve.wait_ge(sem("bc_ps"), 1)
                    ve.tensor_copy(colq[:, 12:16, :, :].rearrange("p a h b -> p (a h b)"), SP_[:, 128:128 + 4 * H * NB])
                    ve.wait_ge(sem("vo_ps"), 1)
                    ve.tensor_copy(colq[:, 0:2, :, :].rearrange("p a h b -> p (a h b)"), SP_[:, 0:2 * H * NB])\
                        .then_inc(sem("oTs"), 1)
                    ve.wait_ge(sem("oTs"), 1)
                    ve.tensor_tensor(colq[:, 3], colq[:, 0], wgT, ALU.mult).then_inc(sem("wv_set"), 1)
                elif step == "SV":
                    ve.wait_ge(sem("gelus"), 1)
                    link(ve.tensor_reduce(sm["mean"][:, :], by_head(vs8), AX.X, ALU.add))
                    link(ve.tensor_scalar(sm["den"][:, :], sm["mean"][:, :], 1.0 / P, None, ALU.mult))
                    link(ve.tensor_tensor(by_head(vs8), by_head(vs8), each_head(sm["den"][:, :]), ALU.subtract))
                    link(ve.tensor_tensor(ta, vs8, vs8, ALU.mult))
                    link(ve.tensor_reduce(sm["mean"][:, :], by_head(ta), AX.X, ALU.add))
                    ve.tensor_scalar(sm["var"][:, :], sm["mean"][:, :], 1.0 / P, EPS, ALU.mult, ALU.add)\
                        .then_inc(sem("vars"), 1)
                elif step == "SH":
                    ve.wait_ge(sem("rvs"), 1)
                    link(ve.tensor_tensor(by_head(vs8), by_head(vs8), each_head(sm["rv"][:, :]), ALU.mult))
                    link(ve.tensor_tensor(vs8, vs8, lnrow[:, 0, :], ALU.mult))
                    link(ve.tensor_tensor(vs8, vs8, lnrow[:, 1, :], ALU.add))
                    ve.sem_inc(sem("vs_new"), 1)
                    link(ve.tensor_tensor(by_head(ta), by_head(vs8), each_head(sm["w00"][:, :]), ALU.mult))
                    link(ve.tensor_tensor(by_head(tb), by_head(ta), each_head(sm["bs0"][:, :]), ALU.add))
                    ve.tensor_tensor(ta, tb, u8, ALU.mult).then_inc(sem("hcm"), 1)
                elif step == "ST":
                    ve.wait_ge(sem("hcm_ps"), 1)
                    ve.tensor_copy(mixTs[:, H:2 * H, :].rearrange("p h b -> p (h b)"), N2[:, 0:H * NB])\
                        .then_inc(sem("hcm_read"), 1)
                elif step == "SQ":
                    ve.wait_ge(sem("C_upd"), NB)
                    ve.tensor_tensor(colq[:, 4], colq[:, 0], sT, ALU.mult)
                    link(ve.scalar_tensor_tensor(out=colq[:, 5], in0=colq[:, 2], scalar=QSCALE, in1=wiT,
                                                 op0=ALU.mult, op1=ALU.mult))
                    link(ve.tensor_tensor(colq[:, 6], colq[:, 4], colq[:, 5], ALU.add))
                    link(ve.tensor_tensor(colq[:, 11], colq[:, 6], rdT, ALU.mult))
                    ve.tensor_tensor(colq[:, 7], colq[:, 11], colq[:, 11], ALU.mult).then_inc(sem("sqml"), 1)
                elif step == "SN":
                    ve.wait_ge(sem("ssml_ps"), 1)
                    ve.tensor_scalar(colq[:, 8].rearrange("p h b -> p (h b)"), N1[:, 0:H * NB], 1.0 / P, EPS,
                                     ALU.mult, ALU.add).then_inc(sem("msml"), 1)
                elif step == "SX":
                    ve.wait_ge(sem("rmls"), 1)
                    ve.wait_ge(sem("sigs"), 1)
                    link(ve.tensor_tensor(colq[:, 6], colq[:, 11], colq[:, 9], ALU.mult))
                    for h in range(H):
                        ins = ve.scalar_tensor_tensor(out=mixTs[:, h, :], in0=colq[:, 6, h, :],
                                                      scalar=prmT[:, PR_HEAD + h:PR_HEAD + h + 1],
                                                      in1=colq[:, 10, h, :], op0=ALU.mult, op1=ALU.mult)
                    link(ins)
                    ve.wait_ge(sem("hcm_read"), 1)
                    link(ve.tensor_copy(s_mix[:, :, 0, :], mixTs[:, :, :]))
                    ve.tensor_tensor(s_mix[:, :, 1, :], mixTs[:, :, :], s_mix[:, :, 0, :].bitcast(F32), ALU.subtract)\
                        .then_inc(sem("s_mix_set"), 1)
                elif step[0] == "C":
                    ve.wait_ge(sem("C_in"), 16)
                    b = int(step[1])
                    ve.wait_ge(sem("qkb"), b + 1)
                    Qb = Q_BANK[b][:, :].rearrange("p (h d) -> p h d", h=H)
                    t0 = tmp[:, 0:HW].rearrange("p (h d) -> p h d", h=H)
                    t1 = tmp[:, HW:2 * HW].rearrange("p (h d) -> p h d", h=H)
                    link(ve.tensor_tensor(t0, C0[:, b], Qb, ALU.mult))
                    ve.tensor_reduce(colq[:, 2, :, b], t0, AX.X, ALU.add)
                    link(ve.tensor_tensor(C0[:, b], C0[:, b], each_head(wiT[:, :, b]), ALU.mult))
                    ve.wait_ge(sem("vk_set"), b + 1)
                    ve.tensor_tensor(C0[:, b], C0[:, b], t1, ALU.add).then_inc(sem("C_upd"), 1)
                    if b == NB - 1:
                        ve.wait_ge(sem("small_out"), 32)

            def split_lo(blk, s, j=0):
                ve.wait_ge(hi_done.sem, hi_done.at(blk, s + 1) + j)
                ve.tensor_tensor(w_lo[:, s % 2], raw[:, s % 2], w_hi[:, s % 2].bitcast(F32),
                                 ALU.subtract).then_inc(lo_done.sem, 1)

            def split_vector(dst_hi, dst_lo, src):
                link(ve.tensor_copy(dst_hi, src))
                return ve.tensor_tensor(dst_lo, src, dst_hi.bitcast(F32), ALU.subtract)

            def norm_tiles(blk, n, ks):
                for k in ks:
                    ve.wait_ge(h32.sem, h32.at(blk, n * KT + k + 1))
                    split_vector(hT_hi[:, k, :], hT_lo[:, k, :], work[:, 2 + k % 2])\
                        .then_inc(h_ready.sem, 1)

            def gate_sum(blk):
                rI, rF, rN = (rows[0:H, i, :] for i in range(3))
                ve.wait_ge(x1_free.sem, x1_free.at(blk, 1))
                ve.memset(R1[:, :], 0.0)
                ve.memset(RT[:, :], 0.0)
                ve.wait_ge(gates_ps.sem, gates_ps.at(blk, 1))
                ve.tensor_scalar(rI, EP_[0:H, :], gb[0:H, :], None, ALU.add)
                link(ve.tensor_scalar(rF, EP_[32:32 + H, :], gb[32:32 + H, :], None, ALU.add))
                ve.scalar_tensor_tensor(out=rN, in0=rF, scalar=-1.0, in1=rF, op0=ALU.mult, op1=ALU.min)\
                    .then_inc(row_n.sem, 1)

            def gate_scans(blk):
                rI, rF, rlf, rL, rb, rM, rbm = (rows[0:H, i, :] for i in (0, 1, 2, 4, 5, 6, 7))
                ve.wait_ge(row_l.sem, row_l.at(blk, 1))
                link(ve.scalar_tensor_tensor(out=rlf, in0=rF, scalar=0.0, in1=rL, op0=ALU.min,
                                             op1=ALU.subtract))
                for c in range(TT):
                    t = slice(c * P, (c + 1) * P)
                    ins = ve.tensor_tensor_scan(rows[0:H, 5, t], onerow[0:H, :], rows[0:H, 2, t], 0.0,
                                                ALU.mult, ALU.add)
                link(ins)
                link(ve.tensor_tensor(RT[0:H, :], rI, rb, ALU.subtract))
                for c in range(TT):
                    t = slice(c * P, (c + 1) * P)
                    last = (c + 1) * P - 1
                    link(ve.tensor_tensor_scan(rows[0:H, 6, t], zrow[:, :], RT[0:H, t], mst[0:H, c:c + 1],
                                               ALU.add, ALU.max))
                    link(ve.tensor_tensor(mst[0:H, c + 1:c + 2], rows[0:H, 5, last:last + 1],
                                          rows[0:H, 6, last:last + 1], ALU.add))
                ve.tensor_scalar(R1[0:H, :], rM, -1.0, None, ALU.mult)
                ve.tensor_tensor(rbm, rb, rM, ALU.add).then_inc(row_m.sem, 1)

            def gate_columns(blk):
                ve.wait_ge(col_ps.sem, col_ps.at(blk, 1))
                ve.tensor_copy(col[:, :, :], SP_[:, :]).then_inc(col_done.sem, 1)
                link(ve.tensor_copy(mst[0:H, 0:1], mst[0:H, TT:TT + 1]))

            def decays(blk):
                ve.wait_ge(wd_ps.sem, wd_ps.at(blk, 1))
                link(ve.tensor_copy(WD[:, :, :].rearrange("p c h -> p (c h)"), T[1][:, 0:TT * H]))
                ve.sem_inc(wd_done.sem, 1)

            heads = lambda ps: ps[:, :].rearrange("p (h e) -> p h e", h=H)

            def chunk_a(blk, c):
                ve.wait_ge(a_done.sem, a_done.at(blk, c + 1))
                ve.wait_ge(e_done.sem, e_done.at(blk, c + 1))
                ve.tensor_tensor(P_sb[:, :, :], E_sb[:, :, :], heads(SP_), ALU.mult).then_inc(p_ready.sem, 1)

            def chunk_b(blk, c):
                wi = col[:, c, 32:32 + H]
                em = col[:, c, 64:64 + H]
                ve.wait_ge(b_done.sem, b_done.at(blk, c + 1))
                ve.tensor_tensor(CT[:, :, :], CT[:, :, :], each_head(WD[:, c, :]), ALU.mult)
                link(ve.tensor_tensor(NT[:, :], NT[:, :], WD[:, c, :], ALU.mult))
                ve.tensor_tensor(CT[:, :, :], CT[:, :, :], heads(T[0]), ALU.add)
                ve.tensor_tensor(NT[:, :], NT[:, :], T[1][:, 0:H], ALU.add).then_inc(ct_done.sem, 1)
                w2 = work[:, 2].rearrange("p (h e) -> p h e", h=H)
                w3 = work[:, 3].rearrange("p (h e) -> p h e", h=H)
                ve.tensor_tensor(w2, heads(N2), each_head(wi), ALU.mult)
                link(ve.tensor_tensor(dd[:, 0, :], EP_[:, H:2 * H], wi, ALU.mult))
                ve.tensor_tensor(hm[:, c], w2, heads(N1), ALU.add).then_inc(num_done.sem, 1)
                link(ve.tensor_tensor(dd[:, 1, :], dd[:, 0, :], EP_[:, 0:H], ALU.add))
                ve.sem_inc(den_read.sem, 1)
                link(ve.scalar_tensor_tensor(out=dd[:, 2, :], in0=dd[:, 1, :], scalar=-1.0,
                                             in1=dd[:, 1, :], op0=ALU.mult, op1=ALU.max))
                link(ve.tensor_tensor(dd[:, 3, :], dd[:, 2, :], em, ALU.max))
                link(ve.reciprocal(dd[:, 0, :], dd[:, 3, :]))
                link(ve.tensor_tensor(hm[:, c], hm[:, c], each_head(dd[:, 0, :]), ALU.mult))
                link(ve.tensor_tensor(w3, hm[:, c], hm[:, c], ALU.mult))
                link(ve.tensor_reduce(SS[:, c, :], w3, AX.X, ALU.add))
                if c == TT - 1:
                    ve.tensor_scalar(SSm[:, :, :], SS[:, :, :], 1.0 / P, EPS, ALU.mult, ALU.add)\
                        .then_inc(ssm_done.sem, 1)

            def vs_stats(blk):
                for c in range(TT):
                    ve.wait_ge(vstr.sem, vstr.at(blk, c + 1))
                    for h in range(H):
                        ve.bn_stats(bst[:, h, :], VST_BANK[c][:, h * P:(h + 1) * P])
                    link(ve.tensor_copy(vs_tm[:, c], heads(VST_BANK[c])))
                    ve.sem_inc(vstm_done.sem, 1)
                    for h in range(H):
                        ins = ve.bn_aggr(MV[:, c, h, :], bst[:, h, :])
                    link(ins)
                v = vs_tm[:, :, :, :].rearrange("p c h e -> p (c h) e")
                mean = MV[:, :, :, 0].rearrange("p c h -> p (c h)")
                ve.tensor_tensor(v, v, each_head(mean), ALU.subtract)
                ve.tensor_scalar(lnv[:, :, :], MV[:, :, :, 1], EPS, None, ALU.add).then_inc(lnv_done.sem, 1)

            def spatial(blk):
                for h in range(H):
                    ve.wait_ge(cms.sem, cms.at(blk, h + 1))
                    out = vsT[:, h, :].rearrange("p (c t) -> p c t", c=TT)
                    ve.scalar_tensor_tensor(out=out, in0=heads(CMS_BANK[h]),
                                            scalar=prmT[:, PR_LNG + h:PR_LNG + h + 1],
                                            in1=bias_cm[:, h, :].unsqueeze(1).broadcast_to([P, TT, P]),
                                            op0=ALU.mult, op1=ALU.add).then_inc(cms_read.sem, 1)

            def gate_u(blk, h):
                ve.wait_ge(evac.sem, evac.at(blk, 5 * H + h + 1))
                ve.wait_ge(cms_read.sem, cms_read.at(blk, h + 1))
                link(ve.tensor_tensor(work[:, h % 2], vsT[:, h, :], uT[:, h, :], ALU.mult))
                split_vector(mix_hi[:, H + h, :], mix_lo[:, H + h, :], work[:, h % 2])\
                    .then_inc(cu_ready.sem, 1)

            def finish_heads(blk):
                ve.wait_ge(so_done.sem, so_done.at(blk, 1))
                for h in range(H):
                    ve.wait_ge(hmtr.sem, hmtr.at(blk, h + 1))
                    link(ve.scalar_tensor_tensor(out=work[:, 2 + h % 2], in0=ML_BANK[h][:, :],
                                                 scalar=prmT[:, PR_HEAD + h:PR_HEAD + h + 1],
                                                 in1=sigT[:, h, :], op0=ALU.mult, op1=ALU.mult))
                    split_vector(mix_hi[:, h, :], mix_lo[:, h, :], work[:, 2 + h % 2])\
                        .then_inc(mix_ready.sem, 1)

            def add(blk, ev, src, u, c, j=0):
                ve.wait_ge(ztr.sem, ztr.at(blk, ev + 1) + j)
                cols = bass.ds(c, P) if not isinstance(c, int) else slice(c, c + P)
                ve.tensor_tensor(x1[:, :, cols], src[:, :, cols], heads(T[u]), ALU.add)\
                    .then_inc(zadd.sem, 1)

            def output(blk, first, slab0, per, src, tiles=None):
                for q in range(per):
                    if tiles is not None and q == per - 1:
                        diagonals(blk, 1)
                    split_lo(blk, slab0 + q + 1)
                if tiles is not None:
                    tiles(range(4))
                with ve.Fori(0, 3) as i:
                    for q in range(per):
                        split_lo(blk, slab0 + per + q + 1, j=i * (2 * per))
                    add(blk, first, src, 0, i * (2 * P), j=i * 2)
                    for q in range(per):
                        split_lo(blk, slab0 + 2 * per + q + 1, j=i * (2 * per))
                    add(blk, first + 1, src, 1, i * (2 * P) + P, j=i * 2)
                for q in range(per):
                    split_lo(blk, slab0 + 7 * per + q + 1)
                if tiles is not None:
                    tiles(range(4, 8))
                add(blk, first + 6, src, 0, 6 * P)
                add(blk, first + 7, src, 1, 7 * P)

            handlers = {"R1": gate_sum, "R3": gate_scans, "COL": gate_columns, "WD": decays,
                        "VST": vs_stats, "CMS": spatial, "ML": finish_heads}

            split_lo(0, 0)
            norm_tiles(0, -1, range(KT))
            split_lo(0, 1)
            round_off(TH_CHAIN)
            def halves(ps, n, out):
                raw_ps = s_ps[:, 0, 0:n, :, :]
                link(ve.tensor_copy(raw_ps, ps[:, 0:n * 2 * NB].rearrange("p (k v b) -> p k v b", v=2, b=NB)))
                link(ve.tensor_tensor(out, raw_ps[:, :, 0, :], raw_ps[:, :, 1, :], ALU.add))

            def sample_residual(ps, gate, src, out):
                halves(ps, KT, s_t[:, :, :])
                link(ve.tensor_tensor(s_t2[:, :, :], s_t[:, :, :], modS[:, gate], ALU.mult))
                link(ve.tensor_tensor(out, s_t2[:, :, :], src, ALU.add))
                ve.tensor_tensor(s_sq[:, :, :], out, out, ALU.mult).then_inc(sem("s_sq"), 1)

            def sample_mean(n):
                ve.wait_ge(sem("s_sum_ps"), n)
                link(ve.tensor_reduce(s_sum[:, :], N1[:, 0:KT * NB].rearrange("p (k b) -> p b k", b=NB),
                                      AX.X, ALU.add))
                ve.tensor_scalar(s_ms[:, :], s_sum[:, :], 1.0 / D, EPS, ALU.mult, ALU.add)\
                    .then_inc(sem("s_mean"), 1)

            def sample_scaled(n, src):
                ve.wait_ge(sem("s_root"), n)
                link(ve.tensor_tensor(s_t[:, :, :], src, s_r[:, :].unsqueeze(1).broadcast_to([P, KT, NB]),
                                      ALU.mult))

            def sample_norm2():
                sample_scaled(1, s_x1[:, :, :])
                link(ve.tensor_tensor(s_t2[:, :, :], s_t[:, :, :], modS[:, 1], ALU.mult))
                link(ve.tensor_tensor(s_h32[:, :, :], s_t2[:, :, :], modS[:, 2], ALU.add))
                split_vector(s_h[:, :, 0, :], s_h[:, :, 1, :], s_h32[:, :, :]).then_inc(sem("s_h_set"), 1)

            def sample_up():
                halves(SP_, FT, s_g[:, :, :])
                halves(EP_, FT, s_u[:, :, :])
                ve.sem_inc(sem("s_up"), 1)
                ve.wait_ge(sem("s_silu"), 1)
                link(ve.tensor_tensor(s_a[:, :, :], s_g[:, :, :], s_u[:, :, :], ALU.mult))
                split_vector(s_act[:, :, 0, :], s_act[:, :, 1, :], s_a[:, :, :]).then_inc(sem("s_act_set"), 1)

            def ve_block(blk, last, first=False):
                at["blk"], at["n"] = blk, 0
                for step in PRE + MIX:
                    if isinstance(step, int):
                        if step + 2 <= N_WIN:
                            split_lo(blk, step + 2)
                        for piece in FIRST.get(step, ()) if first else ():
                            for_samples(piece)
                    elif step in handlers:
                        handlers[step](blk)
                    elif step[0] == "A":
                        chunk_a(blk, int(step[1]))
                    elif step[0] == "B":
                        chunk_b(blk, int(step[1]))
                    elif step[:-1] == "CU":
                        gate_u(blk, int(step[2]))
                output(blk, 0, S_OUT, 1, x_sb)
                if last:
                    sample_residual(N2, 0, xsT[:, :, :], s_x1[:, :, :])
                    sample_mean(1)
                diagonals(blk, 0)
                norm_tiles(blk, 0, range(KT))
                if last:
                    sample_norm2()
                with ve.Fori(0, FT) as i:
                    split_lo(blk, S_UP + 1, j=i * 2)
                    ve.wait_ge(evac.sem, evac.at(blk, N_WIN + N_OUT + 1) + i)
                    ve.tensor_tensor(work[:, 2], work[:, 2], G[0][:, :], ALU.mult).then_inc(silu_done.sem, 1)
                    split_lo(blk, S_UP + 2, j=i * 2)
                    ve.wait_ge(slab_used.sem, slab_used.at(blk, S_UP + 2) + i * 2)
                    ve.wait_ge(silu_done.sem, silu_done.at(blk, 1) + i)
                    ve.tensor_tensor(work[:, 3], work[:, 2], G[1][:, :], ALU.mult).then_inc(gated.sem, 1)
                    ve.wait_ge(act_hi_done.sem, act_hi_done.at(blk, 1) + i)
                    ve.tensor_tensor(act_lo[:, bass.ds(i, 1), :], work[:, 3:4, :],
                                     act_hi[:, bass.ds(i, 1), :].bitcast(F32), ALU.subtract)\
                        .then_inc(act_ready.sem, 1)
                ve.wait_ge(slab_used.sem, slab_used.at(blk, S_DOWN))
                if last:
                    sample_up()
                    ve.wait_ge(sem("fin_ps"), 1)
                    ve.tensor_copy(C_end[:, :, :], heads(N1))
                    ve.tensor_copy(n_end[0:H, :], T[1][0:H, 0:P]).then_inc(sem("fin_set"), 1)
                output(blk, KT, S_DOWN, ND, x1, None if last else lambda ks: norm_tiles(blk, 1, ks))
                if last:
                    sample_residual(N2, 3, s_x1[:, :, :], s_x2[:, :, :])
                    sample_mean(2)
                else:
                    split_lo(blk, NSLAB + 1)
                mean_square(blk, 1 if last else 2, 2 if last else 1)
                for i in range(TT):
                    ins = ve.scalar_tensor_tensor(out=x1[:, i, :], in0=x1[:, i, :], scalar=rrt[:, i:i + 1],
                                                  in1=g_fin[:, :], op0=ALU.mult, op1=ALU.mult)
                    if last:
                        ins.then_inc(sem("y_row"), 1)
                    if last and i == 1:
                        sample_scaled(2, s_x2[:, :, :])
                        ve.tensor_tensor(s_h32[:, :, :], s_t[:, :, :],
                                         each_head(prmT[:, PR_GF:PR_GF + KT], NB), ALU.mult)\
                            .then_inc(sem("s_y_set"), 1)
                if not last:
                    ins.then_inc(y_done.sem, 1)
                    round_off(BLK_CHAIN)

            ve_block(0, False, first=True)
            with ve.Fori(1, NBLK - 1) as blk:
                ve_block(blk, False)
            ve_block(NBLK - 1, True)
            ve.wait_ge(sem("s_y_ps"), 2)
            ve.tensor_copy(s_y[0:NB, BLK:D], NT_BANK[1][0:NB, :]).then_inc(sem("s_done"), 1)

        @block.tensor
        def _(pe):
            mm = pe.matmul
            pe.sem_inc(thin_used.sem, 4)
            pe.wait_ge(sem("consts"), 5)
            pe.wait_ge(sem("c_silu"), 1)
            for k in range(KT):
                ins = pe.transpose(T[0][:, k * R:(k + 1) * R], xs[:, k * P:(k + 1) * P], ident[0:R, 0:R])
            ins.then_inc(sem("cT_ps"), 1)
            pe.wait_ge(sem("cT_set"), 1)

            def thin(t, out, lhs, k0, k1, n, start=True, stop=True, j=None):
                pe.wait_ge(thin_in[t % 4].sem, 16 * (t // 4 + 1) + (0 if j is None else j * 16))
                st = stage_of(t, k1 - k0, n)
                for k in range(k0, k1):
                    ins = mm(out, lhs[:, k, :], st[:, k - k0, :], start=start and k == k0,
                             stop=stop and k == k1 - 1)
                ins.then_inc(thin_used.sem, 1)

            pe.sem_inc(thin_ev.sem, 2)
            with pe.Fori(0, N_ADA // 4 - 1) as i:
                for u in range(4):
                    pe.wait_ge(thin_ev.sem, thin_ev.at(0, u - 1) + i * 4)
                    thin(u, G[u % 2][0:R, :], hTs, 0, KT, 512, j=i)
            def row_columns(row_ready, done):
                pe.wait_ge(sem("xs_in"), 16)
                for k in range(KT):
                    pe.transpose(T[1][:, (KT + k) * NB:(KT + k + 1) * NB], xs[0:NB, k * P:(k + 1) * P],
                                 ident[0:NB, 0:NB])
                pe.wait_ge(sem(row_ready), 1)
                for k in range(KT):
                    ins = pe.transpose(T[1][:, k * NB:(k + 1) * NB], hrow[:, k * P:(k + 1) * P],
                                       ident[0:NB, 0:NB])
                ins.then_inc(sem(done), 1)

            def modulation(t):
                pe.wait_ge(thin_ev.sem, thin_ev.at(0, t - 1))
                thin(t, G[t % 2][0:R, :], hTs, 0, KT, 512)

            modulation(N_ADA - 4)
            modulation(N_ADA - 3)
            row_columns("h1s", "h1T_ps")
            pe.wait_ge(sem("prm_in"), 80)
            pe.transpose(T[0][:, 0:NPR], prm[:, :], ident[0:NPR, 0:NPR]).then_inc(sem("prm_ps"), 1)
            pe.wait_ge(sem("ws_masked"), 1)
            for h in range(H):
                ins = pe.transpose(N1[:, h * P:(h + 1) * P], w_raw[:, h, :], ident[:, :])
            ins.then_inc(sem("wT_ps"), 1)
            modulation(N_ADA - 2)
            pe.wait_ge(sem("wT_set"), 1)
            pe.wait_ge(sem("ones"), 1)
            mm(N2[0:1, :], onecol[:, :], wT[:, :, :].rearrange("s h t -> s (h t)"), start=True, stop=True)\
                .then_inc(sem("rsum_ps"), 1)
            modulation(N_ADA - 1)
            pe.wait_ge(sem("rsum_set"), 1)
            pe.wait_ge(sem("cmb_in"), 32)
            for h in range(H):
                ins = mm(EP_[:, h * P:(h + 1) * P], lnb_lh[:, h, :], cmb_rh[:, h, :], start=True, stop=True)
            ins.then_inc(sem("bcm_ps"), 1)


            def modulation_columns():
                pe.wait_ge(thin_ev.sem, thin_ev.at(0, N_ADA))
                for j in range(NMOD * KT):
                    ins = pe.transpose(SP_[:, j * R:(j + 1) * R], mod[:, j * P:(j + 1) * P], ident[0:R, 0:R])
                ins.then_inc(sem("modT_ps"), 1)

            for j, (c, n) in enumerate(thin_in_cols):
                t = TH_IN + j
                pe.wait_ge(thin_ev.sem, thin_ev.at(0, t - 1))
                if j == 0:
                    pe.wait_ge(sem("h1T_set"), 1)
                thin(t, G[t % 2][0:NB, 0:n], h1T, 0, KT, n)
                if j == 1:
                    modulation_columns()
            def for_samples(step):
                if step == "SG":
                    pe.wait_ge(sem("proj_set"), 1)
                    for i, c0 in enumerate((V0, O0)):
                        for h in range(H):
                            ins = pe.transpose(SP_[:, (i * H + h) * NB:(i * H + h + 1) * NB],
                                               proj[:, c0 + h * P:c0 + (h + 1) * P], ident[0:NB, 0:NB])
                    ins.then_inc(sem("vo_ps"), 1)
                elif step == "SC":
                    pe.wait_ge(sem("bcx_set"), 1)
                    mm(SP_[:, 128:128 + 4 * H * NB], onerow[0:NB, :],
                       bcx[:, :, :, :].rearrange("p a h b -> p (a h b)"), start=True, stop=True)\
                        .then_inc(sem("bc_ps"), 1)
                elif step == "ST":
                    pe.wait_ge(sem("C_upd"), NB)
                    pe.wait_ge(sem("hcm"), 1)
                    for h in range(H):
                        ins = pe.transpose(N2[:, h * NB:(h + 1) * NB], hrow[:, h * P:(h + 1) * P], ident[0:NB, 0:NB])
                    ins.then_inc(sem("hcm_ps"), 1)
                elif step == "SN":
                    pe.wait_ge(sem("sqml"), 1)
                    mm(N1[:, 0:H * NB], onerow[:, :], colq[:, 7].rearrange("p h b -> p (h b)"), start=True,
                       stop=True).then_inc(sem("ssml_ps"), 1)
                elif step[0] == "C":
                    b = int(step[1])
                    if b == 0:
                        pe.wait_ge(sem("sel8_set"), 1)
                    else:
                        pe.wait_ge(sem("C_upd"), 7 if b == 7 else max(b - 1, 1))
                    mm(Q_BANK[b][:, :], sel8[:, b, :], proj[:, Q0:Q0 + HW], start=True, stop=True)
                    mm(K_BANK[b][:, :], sel8[:, b, :], proj[:, K0:K0 + HW], start=True, stop=True)\
                        .then_inc(sem("qkb"), 1)

            pe.sem_inc(slab_used.sem, 1)
            pe.sem_inc(ztr.sem, 2)

            def product(out, slot, rhs_hi, rhs_lo, tiles, start=True, stop=True, before_tile=None):
                for n, (k, r) in enumerate(tiles):
                    if before_tile is not None:
                        before_tile(k)
                    last = n == len(tiles) - 1
                    mm(out, w_lo[:, slot, k, :], rhs_hi[:, r, :], start=start and n == 0, stop=False)
                    mm(out, w_hi[:, slot, k, :], rhs_lo[:, r, :], start=False, stop=False)
                    ins = mm(out, w_hi[:, slot, k, :], rhs_hi[:, r, :], start=False, stop=stop and last)
                return ins

            every = [(k, k) for k in range(KT)]

            def sample_product(out, slot, rhs, tiles, start=True, stop=True):
                for n, (k, r) in enumerate(tiles):
                    mm(out, w_lo[:, slot, k, :], rhs[:, r, :, :], start=start and n == 0, stop=False)
                    ins = mm(out, w_hi[:, slot, k, :], rhs[:, r, :, :], start=False,
                             stop=stop and n == len(tiles) - 1)
                return ins

            def sample_sum():
                pe.wait_ge(sem("s_sq"), sums_done[0] + 1)
                mm(N1[:, 0:KT * NB], onerow[:, :], s_sq[:, :, :].rearrange("p k b -> p (k b)"), start=True,
                   stop=True).then_inc(sem("s_sum_ps"), 1)
                sums_done[0] += 1

            sums_done = [0]

            def slab_ready(blk, s, j=0):
                pe.wait_ge(lo_done.sem, lo_done.at(blk, s + 1) + j)

            def norm_out(blk, n, x_tiles, ks):
                pe.wait_ge(dg_done.sem, dg_done.at(blk, n + 1))
                for k in ks:
                    if k >= 4:
                        pe.wait_ge(h32.sem, h32.at(blk, n * KT + k - 3))
                    for i in range(TT):
                        ins = mm(NT_BANK[k % 4][:, i * P:(i + 1) * P], x_tiles[:, i, k * P:(k + 1) * P],
                                 dg[:, i, :], start=True, stop=True)
                    ins.then_inc(trx.sem, 1)

            def gates(blk):
                pe.wait_ge(h32.sem, h32.at(blk, 0))
                for k in range(KT):
                    w = slice(36 * k, 36 * k + P)
                    pe.wait_ge(h_ready.sem, h_ready.at(blk, k + 1 - KT))
                    mm(EP_[:, :], gw_lo[:, w], hT_hi[:, k, :], start=k == 0, stop=False)
                    mm(EP_[:, :], gw_hi[:, w], hT_lo[:, k, :], start=False, stop=False)
                    ins = mm(EP_[:, :], gw_hi[:, w], hT_hi[:, k, :], start=False, stop=k == KT - 1)
                ins.then_inc(gates_ps.sem, 1)

            def columns(blk):
                pe.wait_ge(rt_ready.sem, rt_ready.at(blk, 1))
                for c in range(TT):
                    ins = pe.transpose(SP_[:, c * P:(c + 1) * P], RT[:, c * P:(c + 1) * P], ident[:, :])
                ins.then_inc(col_ps.sem, 1)

            def decays(blk):
                pe.wait_ge(col_done.sem, col_done.at(blk, 1))
                pe.wait_ge(vtm_done.sem, vtm_done.at(blk, TT))
                mm(T[1][:, 0:TT * H], last_row[:, :], col[:, :, 32:32 + H], start=True, stop=True)\
                    .then_inc(wd_ps.sem, 1)

            def by_tokens(done, src, c, out):
                for h in range(H):
                    ins = pe.transpose(out[:, h * P:(h + 1) * P], src[:, h, c * P:(c + 1) * P],
                                       ident[:, :])
                ins.then_inc(done.sem, 1)

            def v_tokens(blk, c):
                if c == 0:
                    pe.wait_ge(evac.sem, evac.at(blk, H))
                if c >= 2:
                    pe.wait_ge(vtm_done.sem, vtm_done.at(blk, c - 1))
                by_tokens(vtr, vT, c, T[c % 2])

            def chunk_a(blk, c):
                t = slice(c * P, (c + 1) * P)
                if c == 0:
                    pe.wait_ge(evac.sem, evac.at(blk, 3 * H))
                    pe.wait_ge(wd_done.sem, wd_done.at(blk, 1))
                else:
                    pe.wait_ge(ct_done.sem, ct_done.at(blk, c))
                    pe.wait_ge(den_read.sem, den_read.at(blk, c))
                    pe.wait_ge(p_ready.sem, p_ready.at(blk, c))
                if c == 3:
                    pe.wait_ge(vstm_done.sem, vstm_done.at(blk, 1))
                by_tokens(ktr, kT, c, T[0])
                mm(EP_[:, :], identb[:, :], mask[:, :].unsqueeze(1).broadcast_to([P, H, P]), start=True,
                   stop=False)
                for h in range(H):
                    mm(EP_[:, h * P:(h + 1) * P], sel[:, h, :], R1[:, t], start=False, stop=h == H - 1)
                for h in range(H):
                    ins = mm(SP_[:, h * P:(h + 1) * P], kT[:, h, t], qT[:, h, t], start=True, stop=True)
                ins.then_inc(a_done.sem, 1)

            def chunk_b(blk, c):
                t = slice(c * P, (c + 1) * P)
                if c > 0:
                    pe.wait_ge(num_done.sem, num_done.at(blk, c))
                pe.wait_ge(p_ready.sem, p_ready.at(blk, c + 1))
                if c == 3:
                    pe.wait_ge(vstm_done.sem, vstm_done.at(blk, TT))
                for h in range(H):
                    mm(N1[:, h * P:(h + 1) * P], P_sb[:, h, :], v_tm[:, c, h, :], start=True, stop=True)
                    mm(EP_[:, h:h + 1], P_sb[:, h, :], onecol[:, :], start=True, stop=True)
                pe.wait_ge(ct_done.sem, ct_done.at(blk, c))
                for h in range(H):
                    mm(N2[:, h * P:(h + 1) * P], qT[:, h, t], CT[:, h, :], start=True, stop=True)
                    mm(EP_[:, H + h:H + h + 1], qT[:, h, t], NT[:, h:h + 1], start=True, stop=True)
                pe.wait_ge(vg_done.sem, vg_done.at(blk, c + 1))
                pe.wait_ge(ktm_done.sem, ktm_done.at(blk, c + 1))
                for h in range(H):
                    mm(T[0][:, h * P:(h + 1) * P], k_tm[:, h, :], vg[:, h, :], start=True, stop=True)
                    ins = mm(T[1][:, h:h + 1], k_tm[:, h, :], col[:, c, 96 + h:97 + h], start=True,
                             stop=True)
                ins.then_inc(b_done.sem, 1)

            def vs_tokens(blk):
                pe.wait_ge(gv_done.sem, gv_done.at(blk, 1))
                pe.wait_ge(ct_done.sem, ct_done.at(blk, 3))
                pe.wait_ge(num_done.sem, num_done.at(blk, 3))
                for c in range(TT):
                    by_tokens(vstr, vsT, c, VST_BANK[c])

            def spatial(blk):
                pe.wait_ge(vn_done.sem, vn_done.at(blk, 1))
                pe.wait_ge(num_done.sem, num_done.at(blk, TT))
                pe.wait_ge(den_read.sem, den_read.at(blk, TT))
                for h in range(H):
                    for c in range(TT):
                        ins = mm(CMS_BANK[h][:, c * P:(c + 1) * P], vs_tm[:, c, h, :], wT[:, h, :],
                                 start=True, stop=True)
                    ins.then_inc(cms.sem, 1)

            def finish_heads(blk):
                pe.wait_ge(hm_done.sem, hm_done.at(blk, 1))
                pe.wait_ge(ct_done.sem, ct_done.at(blk, TT))
                pe.wait_ge(cms_read.sem, cms_read.at(blk, 2))
                for h in range(H):
                    for c in range(TT):
                        ins = pe.transpose(ML_BANK[h][:, c * P:(c + 1) * P], hm[:, c, h, :], ident[:, :])
                    ins.then_inc(hmtr.sem, 1)

            def mix_slab(blk, s):
                slab_ready(blk, s)
                pe.wait_ge(evac.sem, evac.at(blk, max(s - 1, 0)))
                product(G[s % 2][:, :], s % 2, hT_hi, hT_lo, every).then_inc(slab_used.sem, 1)

            def to_tokens(blk, ev, u, n_ev, j=0):
                pe.wait_ge(evac.sem, evac.at(blk, n_ev) + j)
                pe.wait_ge(zadd.sem, zadd.at(blk, ev - 1) + j)
                for i in range(TT):
                    ins = pe.transpose(T[u][:, i * P:(i + 1) * P], work[:, u, i * P:(i + 1) * P],
                                       ident[:, :])
                ins.then_inc(ztr.sem, 1)

            def output(blk, first, e0, gemm, tiles=None):
                gemm(0, 0, 0)
                if tiles is not None:
                    tiles(range(4))
                with pe.Fori(0, 3) as i:
                    gemm(1, 1, i)
                    to_tokens(blk, first, 0, e0 + 1, j=i * 2)
                    gemm(2, 0, i)
                    to_tokens(blk, first + 1, 1, e0 + 2, j=i * 2)
                gemm(7, 1, 0)
                if tiles is not None:
                    tiles(range(4, 8))
                to_tokens(blk, first + 6, 0, e0 + 7)
                to_tokens(blk, first + 7, 1, e0 + 8)

            pe.sem_inc(zadd.sem, 2)
            pe.sem_inc(h_ready.sem, 2)
            pe.sem_inc(evac.sem, 1)
            pe.sem_inc(gated.sem, 1)
            pe.sem_inc(silu_done.sem, 1)
            pe.sem_inc(ct_done.sem, 1)
            handlers = {"R1": gates, "COL": columns, "WD": decays, "VST": vs_tokens, "CMS": spatial,
                        "ML": finish_heads}
            norm_out(0, -1, x_sb, range(KT))
            def pe_block(blk, last, first=False):
                if last:
                    pe.wait_ge(sem("s_mix_set"), 1)
                gates(blk)
                for step in PRE + MIX:
                    if isinstance(step, int):
                        mix_slab(blk, step)
                        for piece in FIRST.get(step, ()) if first else ():
                            for_samples(piece)
                    elif step in ("COL", "WD", "VST", "CMS", "ML"):
                        handlers[step](blk)
                    elif step[0] == "V":
                        v_tokens(blk, int(step[1]))
                    elif step[0] == "A":
                        chunk_a(blk, int(step[1]))
                    elif step[0] == "B":
                        chunk_b(blk, int(step[1]))

                def s_columns(ps, n, j):
                    return ps[:, bass.ds(j * (2 * NB) + n * (2 * NB), 2 * NB)]

                def out_gemm(n, u, i):
                    slab_ready(blk, S_OUT + n, i * 2)
                    pe.wait_ge(evac.sem, evac.at(blk, S_OUT + n - 1) + i * 2)
                    ready = None
                    if n == 0:
                        def ready(k):
                            done = mix_ready if k < H else cu_ready
                            pe.wait_ge(done.sem, done.at(blk, k % H + 1))
                    ins = product(G[u][:, :], u, mix_hi, mix_lo, every, before_tile=ready)
                    if last:
                        ins = sample_product(s_columns(N2, n, i * 2), u, s_mix, every)
                    ins.then_inc(slab_used.sem, 1)

                output(blk, 0, N_WIN, out_gemm)
                if last:
                    sample_sum()
                    pe.wait_ge(sem("s_mean"), 1)
                norm_out(blk, 0, x1, range(KT))
                with pe.Fori(0, FT // 2) as half_i:
                    for pair in range(2):
                        slabs, n = half_i * 4, half_i * 2
                        slab_ready(blk, S_UP + 2 * pair, slabs)
                        pe.wait_ge(evac.sem, evac.at(blk, N_WIN + N_OUT + pair) + n)
                        pe.wait_ge(silu_done.sem, silu_done.at(blk, pair) + n)
                        ins = product(G[0][:, :], 0, hT_hi, hT_lo, every,
                                      before_tile=lambda k: pe.wait_ge(h_ready.sem, h_ready.at(blk, k + 1)))
                        if last:
                            pe.wait_ge(sem("s_h_set"), 1)
                            ins = sample_product(s_columns(SP_, pair, n), 0, s_h, every)
                        ins.then_inc(slab_used.sem, 1)
                        slab_ready(blk, S_UP + 2 * pair + 1, slabs)
                        pe.wait_ge(gated.sem, gated.at(blk, pair) + n)
                        ins = product(G[1][:, :], 1, hT_hi, hT_lo, every)
                        if last:
                            ins = sample_product(s_columns(EP_, pair, n), 1, s_h, every)
                        ins.then_inc(slab_used.sem, 1)

                def down_gemm(n, u, i):
                    pe.wait_ge(evac.sem, evac.at(blk, N_WIN + N_OUT + FT + n - 1) + i * 2)
                    for q, (k0, k1) in enumerate(DOWN_K):
                        slab_ready(blk, S_DOWN + ND * n + q, i * (2 * ND))
                        tiles = [(k - k0, k) for k in range(k0, k1)]
                        ready = None
                        if n == 0:
                            def ready(k, k0=k0):
                                pe.wait_ge(act_ready.sem, act_ready.at(blk, k0 + k + 1))
                        ins = product(G[u][:, :], q % 2, act_hi, act_lo, tiles, start=q == 0,
                                      stop=q == ND - 1, before_tile=ready)
                        if last:
                            if n == 0 and q == 0:
                                pe.wait_ge(sem("s_act_set"), 1)
                            ins = sample_product(s_columns(N2, n, i * 2), q % 2, s_act, tiles,
                                                 start=q == 0, stop=q == ND - 1)
                        ins.then_inc(slab_used.sem, 1)

                if last:
                    for h in range(H):
                        pe.transpose(N1[:, h * P:(h + 1) * P], CT[:, h, :], ident[:, :])
                    pe.transpose(T[1][0:H, 0:P], NT[:, :], ident[:, :]).then_inc(sem("fin_ps"), 1)
                output(blk, KT, N_WIN + N_OUT + FT, down_gemm,
                       None if last else lambda ks: norm_out(blk, 1, x_sb, ks))
                if last:
                    sample_sum()

            pe_block(0, False, first=True)
            with pe.Fori(1, NBLK - 1) as blk:
                pe_block(blk, False)
            pe_block(NBLK - 1, True)
            pe.wait_ge(sem("s_y_set"), 1)
            for k in range(KT):
                ins = pe.transpose(NT_BANK[k // 4][0:NB, (k % 4) * P:(k % 4 + 1) * P], s_h32[:, k, :],
                                   ident[:, :])
                if k % 4 == 3:
                    ins.then_inc(sem("s_y_ps"), 1)


_INS = ["x_prompt", "x_sample", "c_prompt", "c_sample", "state_mlstm_C", "state_mlstm_n", "state_mlstm_m",
        "w_ada", "b_ada", "g_norm1", "w_in", "b_gate", "g_mlstm_head", "ln_v_g", "ln_v_b", "w_s", "b_s",
        "w_out", "g_norm2", "w_gate_up", "w_down", "g_final"]
_OUTS = [(1, SEQ, D), (NB, 1, D), (1, 1, H, P, P), (1, 1, H, P), (1, 1, H), (1, NB, H, P, P),
         (1, NB, H, P), (1, NB, H), (1, NB, 1, H, P)]


def kernel(**inputs):
    import numpy as _np
    import concourse.bacc as _bacc
    from concourse import mybir as _mybir
    from concourse.bass_utils import run_bass_kernel_spmd as _run

    nc = _bacc.Bacc("TRN2", target_bir_lowering=False, num_devices=1)
    arrays, args = {}, []
    for name in _INS:
        a = _np.ascontiguousarray(inputs[name])
        arrays[f"in_{name}_dram"] = a
        args.append(nc.dram_tensor(f"in_{name}_dram", a.shape, _mybir.dt.from_np(a.dtype),
                                   kind="ExternalInput").ap())
    for i, shape in enumerate(_OUTS):
        args.append(nc.dram_tensor(f"out_{i}_dram", shape, _mybir.dt.float32, kind="ExternalOutput").ap())
    hybrid_step(nc, *args)
    r = _run(nc, [arrays], core_ids=[0])
    return tuple(r.results[0][f"out_{i}_dram"] for i in range(len(_OUTS)))
```
